# Optimizing a Trainium2 kernel written in Bass

```python
import jax, jax.numpy as jnp
from jax import lax
import numpy as np

D_MODEL = 2048
BATCH = 1
SEQ = 256
DEPTH = 2

HEAD_DIM = 128
MLA_HEADS = 4
MLA_Q_LORA = 512
MLA_KV_LORA = 256
MLA_NOPE = 128
MLA_ROPE = 64
MLA_V = 128
FOX_HEADS = 4
NSA_HEADS = 8
NSA_KV_GROUPS = 2
NSA_GQA = NSA_HEADS // NSA_KV_GROUPS
NSA_CMP_LEN = 32
NSA_CMP_STRIDE = 16
NSA_CMP_HIDDEN = 512
NSA_SLC_BLOCK = 64
NSA_TOPK = 16
NSA_WINDOW = 512
NSA_SLC_Q_BLOCK = 64
W_MLA = MLA_HEADS * MLA_V
W_FOX = FOX_HEADS * HEAD_DIM
W_NSA = NSA_HEADS * HEAD_DIM
D_MIX = W_MLA + W_FOX + W_NSA
NSA_KV = NSA_KV_GROUPS * HEAD_DIM
IN_SPLITS = (MLA_Q_LORA, MLA_KV_LORA, MLA_ROPE,
             W_FOX, W_FOX, W_FOX, FOX_HEADS,
             W_NSA, NSA_KV, NSA_KV, NSA_KV, NSA_KV, NSA_KV, NSA_KV, 3 * NSA_HEADS)
IN_COLS = sum(IN_SPLITS)
Q_BLOCK = 128
ROPE_THETA = 500000.0
PARTIAL_ROT = HEAD_DIM // 4
D_FF = 4 * D_MODEL
MAX_POS_OFFSET = 1024
EPS = 1e-6
NEG = -1e30
BIG = 1e30

kernel_name = 'hybrid_mla_fox_nsa_block'

f32 = jnp.float32

def rms_norm(x, gain):
    x32 = x.astype(f32)
    y = x32 * lax.rsqrt(jnp.mean(x32 * x32, axis=-1, keepdims=True) + EPS)
    return (y * gain.astype(f32)).astype(x.dtype)

def rotary(x, positions, rot_dim):
    half = rot_dim // 2
    inv_freq = ROPE_THETA ** (-jnp.arange(half, dtype=f32) / half)
    ang = positions.astype(f32)[..., None] * inv_freq
    ang = ang.reshape(ang.shape[:2] + (1,) * (x.ndim - 3) + (half,))
    cos, sin = jnp.cos(ang), jnp.sin(ang)
    xf = x.astype(f32)
    x1, x2, rest = xf[..., :half], xf[..., half:rot_dim], xf[..., rot_dim:]
    out = jnp.concatenate([x1 * cos - x2 * sin, x2 * cos + x1 * sin, rest], axis=-1)
    return out.astype(x.dtype)

def causal_block_attention(q, k, v, scale, decay=None):
    B, S, H, Dk = q.shape
    nb = S // Q_BLOCK
    key_pos = jnp.arange(S)
    qb = q.reshape(B, nb, Q_BLOCK, H, Dk).swapaxes(0, 1)
    xs = (jnp.arange(nb), qb)
    if decay is not None:
        dk_all = decay.transpose(0, 2, 1)
        xs = xs + (decay.reshape(B, nb, Q_BLOCK, H).swapaxes(0, 1),)

    def block(args):
        i, q_blk = args[0], args[1]
        s = jnp.einsum('bqhd,bkhd->bhqk', q_blk, k).astype(f32) * scale
        if decay is not None:
            s = s + args[2].transpose(0, 2, 1)[..., None] - dk_all[:, :, None, :]
        qpos = i * Q_BLOCK + jnp.arange(Q_BLOCK)
        s = jnp.where(key_pos[None, :] <= qpos[:, None], s, NEG)
        p = jax.nn.softmax(s, axis=-1).astype(v.dtype)
        return jnp.einsum('bhqk,bkhd->bqhd', p, v)

    o = lax.map(block, xs)
    return o.swapaxes(0, 1).reshape(B, S, H, v.shape[-1])

def mla_mixer(cq, ckv, kr, positions, q_norm, w_uq, kv_norm, w_ukv):
    B, S, _ = cq.shape
    q = (rms_norm(cq, q_norm) @ w_uq).reshape(B, S, MLA_HEADS, MLA_NOPE + MLA_ROPE)
    kv = (rms_norm(ckv, kv_norm) @ w_ukv).reshape(B, S, MLA_HEADS, MLA_NOPE + MLA_V)
    q_rope = rotary(q[..., MLA_NOPE:], positions, MLA_ROPE)
    k_rope = rotary(kr, positions, MLA_ROPE)
    q_full = jnp.concatenate([q[..., :MLA_NOPE], q_rope], axis=-1)
    k_full = jnp.concatenate(
        [kv[..., :MLA_NOPE], jnp.broadcast_to(k_rope[:, :, None, :], (B, S, MLA_HEADS, MLA_ROPE))], axis=-1)
    o = causal_block_attention(q_full, k_full, kv[..., MLA_NOPE:], (MLA_NOPE + MLA_ROPE) ** -0.5)
    return o.reshape(B, S, W_MLA)

def fox_mixer(q, k, v, f_logit, b_f):
    B, S, _ = q.shape
    shp = (B, S, FOX_HEADS, HEAD_DIM)
    log_f = jax.nn.log_sigmoid(f_logit.astype(f32) + b_f.astype(f32))
    cum = lax.cumsum(log_f, axis=1)
    o = causal_block_attention(q.reshape(shp), k.reshape(shp), v.reshape(shp), HEAD_DIM ** -0.5, decay=cum)
    return o.reshape(B, S, W_FOX)

def nsa_compress(tok, pos_emb, w1, w2):
    B, S, G, D = tok.shape
    n_cmp = (S - NSA_CMP_LEN) // NSA_CMP_STRIDE + 1
    idx = np.arange(n_cmp)[:, None] * NSA_CMP_STRIDE + np.arange(NSA_CMP_LEN)[None, :]
    blk = tok[:, idx] + pos_emb[None, None, :, None, :]
    blk = blk.transpose(0, 1, 3, 2, 4).reshape(B, n_cmp, G, NSA_CMP_LEN * D)
    return jax.nn.gelu(blk @ w1) @ w2

def nsa_cmp_slc(q, k_cmp, v_cmp, k_slc, v_slc):
    B, S, G, Hg, D = q.shape
    n_cmp = k_cmp.shape[1]
    n_slc = S // NSA_SLC_BLOCK
    top_k = min(NSA_TOPK, n_slc)
    scale = D ** -0.5
    c_start = np.arange(n_cmp) * NSA_CMP_STRIDE
    cmp_end = jnp.asarray(c_start + NSA_CMP_LEN - 1)
    s_start = np.arange(n_slc) * NSA_SLC_BLOCK
    ov = np.minimum(c_start[:, None] + NSA_CMP_LEN, s_start[None, :] + NSA_SLC_BLOCK) - np.maximum(c_start[:, None], s_start[None, :])
    overlap = jnp.asarray((np.clip(ov, 0, None) / NSA_CMP_LEN).astype(np.float32))
    k_sb = k_slc.reshape(B, n_slc, NSA_SLC_BLOCK, G, D).transpose(0, 3, 1, 2, 4)
    v_sb = v_slc.reshape(B, n_slc, NSA_SLC_BLOCK, G, D).transpose(0, 3, 1, 2, 4)
    nq = S // NSA_SLC_Q_BLOCK
    qc = q.reshape(B, nq, NSA_SLC_Q_BLOCK, G, Hg, D).swapaxes(0, 1)
    b_ix = jnp.arange(B)[:, None, None, None]
    g_ix = jnp.arange(G)[None, :, None, None]
    j = jnp.arange(n_slc)

    def chunk(args):
        i, q_c = args
        t = i * NSA_SLC_Q_BLOCK + jnp.arange(NSA_SLC_Q_BLOCK)
        s = jnp.einsum('bqghd,bngd->bghqn', q_c, k_cmp).astype(f32) * scale
        valid = cmp_end[None, :] <= t[:, None]
        s = jnp.where(valid, s, NEG)
        p = jax.nn.softmax(s, axis=-1) * jnp.any(valid, axis=-1)[:, None].astype(f32)
        o_cmp = jnp.einsum('bghqn,bngd->bqghd', p.astype(v_cmp.dtype), v_cmp)
        imp = jnp.einsum('bghqn,nm->bgqm', p, overlap)
        cur = t // NSA_SLC_BLOCK
        forced = (j[None, :] == 0) | (j[None, :] == cur[:, None]) | (j[None, :] == cur[:, None] - 1)
        future = j[None, :] > cur[:, None]
        imp = jnp.where(forced, BIG, jnp.where(future, NEG, imp))
        _, sel = lax.top_k(imp, top_k)
        sel_ok = sel <= cur[None, None, :, None]
        k_g = k_sb[b_ix, g_ix, sel]
        v_g = v_sb[b_ix, g_ix, sel]
        tok = sel[..., None] * NSA_SLC_BLOCK + jnp.arange(NSA_SLC_BLOCK)
        m = (tok <= t[None, None, :, None, None]) & sel_ok[..., None]
        s2 = jnp.einsum('bqghd,bgqksd->bgqhks', q_c, k_g).astype(f32) * scale
        s2 = jnp.where(m[:, :, :, None], s2, NEG).reshape(B, G, NSA_SLC_Q_BLOCK, Hg, top_k * NSA_SLC_BLOCK)
        p2 = jax.nn.softmax(s2, axis=-1).astype(v_g.dtype).reshape(B, G, NSA_SLC_Q_BLOCK, Hg, top_k, NSA_SLC_BLOCK)
        o_slc = jnp.einsum('bgqhks,bgqksd->bqghd', p2, v_g)
        return o_cmp, o_slc

    o_cmp, o_slc = lax.map(chunk, (jnp.arange(nq), qc))
    return (o_cmp.swapaxes(0, 1).reshape(B, S, G, Hg, D),
            o_slc.swapaxes(0, 1).reshape(B, S, G, Hg, D))

def nsa_window(q, k, v):
    B, S, G, Hg, D = q.shape
    span = NSA_WINDOW + Q_BLOCK
    kp = jnp.pad(k, ((0, 0), (NSA_WINDOW, 0), (0, 0), (0, 0)))
    vp = jnp.pad(v, ((0, 0), (NSA_WINDOW, 0), (0, 0), (0, 0)))
    nb = S // Q_BLOCK
    qb = q.reshape(B, nb, Q_BLOCK, G, Hg, D).swapaxes(0, 1)

    def block(args):
        i, q_blk = args
        start = i * Q_BLOCK
        k_blk = lax.dynamic_slice_in_dim(kp, start, span, axis=1)
        v_blk = lax.dynamic_slice_in_dim(vp, start, span, axis=1)
        t = start + jnp.arange(Q_BLOCK)
        s_pos = start - NSA_WINDOW + jnp.arange(span)
        m = (s_pos[None, :] <= t[:, None]) & (t[:, None] - s_pos[None, :] < NSA_WINDOW) & (s_pos[None, :] >= 0)
        s = jnp.einsum('bqghd,bkgd->bghqk', q_blk, k_blk).astype(f32) * (D ** -0.5)
        s = jnp.where(m, s, NEG)
        p = jax.nn.softmax(s, axis=-1).astype(v_blk.dtype)
        return jnp.einsum('bghqk,bkgd->bqghd', p, v_blk)

    o = lax.map(block, (jnp.arange(nb), qb))
    return o.swapaxes(0, 1).reshape(B, S, G, Hg, D)

def nsa_mixer(q, kc, vc, ks, vs, kw, vw, gate_logit, positions, pos_k, pos_v, ck_w1, ck_w2, cv_w1, cv_w2):
    B, S, _ = q.shape
    kv_shape = (B, S, NSA_KV_GROUPS, HEAD_DIM)
    q = rotary(q.reshape(B, S, NSA_KV_GROUPS, NSA_GQA, HEAD_DIM), positions, PARTIAL_ROT)
    kc = rotary(kc.reshape(kv_shape), positions, PARTIAL_ROT)
    ks = rotary(ks.reshape(kv_shape), positions, PARTIAL_ROT)
    kw = rotary(kw.reshape(kv_shape), positions, PARTIAL_ROT)
    k_cmp = nsa_compress(kc, pos_k, ck_w1, ck_w2)
    v_cmp = nsa_compress(vc.reshape(kv_shape), pos_v, cv_w1, cv_w2)
    o_cmp, o_slc = nsa_cmp_slc(q, k_cmp, v_cmp, ks, vs.reshape(kv_shape))
    o_win = nsa_window(q, kw, vw.reshape(kv_shape))
    g = jax.nn.sigmoid(gate_logit.astype(f32)).reshape(B, S, NSA_KV_GROUPS, NSA_GQA, 3).astype(q.dtype)
    o = g[..., 0:1] * o_cmp + g[..., 1:2] * o_slc + g[..., 2:3] * o_win
    return o.reshape(B, S, W_NSA)

def hybrid_layer(x, c_act, positions, ada_w, ada_b, norm_mix, norm_mlp, w_in, fox_b_f,
                 mla_q_norm, mla_w_uq, mla_kv_norm, mla_w_ukv,
                 nsa_pos_k, nsa_pos_v, nsa_cmp_k_w1, nsa_cmp_k_w2, nsa_cmp_v_w1, nsa_cmp_v_w2,
                 out_norm, w_out, mlp_w1, mlp_w2):
    mod = c_act @ ada_w + ada_b
    sh_a, sc_a, gt_a, sh_m, sc_m, gt_m = jnp.split(mod[:, None, :], 6, axis=-1)
    h = rms_norm(x, norm_mix) * (1.0 + sc_a) + sh_a
    split_points = np.cumsum(IN_SPLITS)[:-1].tolist()
    (cq, ckv, kr, fq, fk, fv, ff,
     nq, nkc, nvc, nks, nvs, nkw, nvw, ng) = jnp.split(h @ w_in, split_points, axis=-1)
    o_mla = mla_mixer(cq, ckv, kr, positions, mla_q_norm, mla_w_uq, mla_kv_norm, mla_w_ukv)
    o_fox = fox_mixer(fq, fk, fv, ff, fox_b_f)
    o_nsa = nsa_mixer(nq, nkc, nvc, nks, nvs, nkw, nvw, ng, positions,
                      nsa_pos_k, nsa_pos_v, nsa_cmp_k_w1, nsa_cmp_k_w2, nsa_cmp_v_w1, nsa_cmp_v_w2)
    g_mla, g_fox, g_nsa = jnp.split(out_norm, [W_MLA, W_MLA + W_FOX])
    o = jnp.concatenate([rms_norm(o_mla, g_mla), rms_norm(o_fox, g_fox), rms_norm(o_nsa, g_nsa)], axis=-1)
    x = x + gt_a * (o @ w_out)
    h = rms_norm(x, norm_mlp) * (1.0 + sc_m) + sh_m
    u = jnp.square(jax.nn.relu(h @ mlp_w1))
    return x + gt_m * (u @ mlp_w2)

def setup_inputs(seed: int = 0) -> dict:
    key = jax.random.key(seed)
    ks = iter(jax.random.split(key, 32))

    def dense(shape, fan_in, s=1.0):
        return jax.random.normal(next(ks), shape, f32) * (s * fan_in ** -0.5)

    def gain(shape):
        return 1.0 + 0.02 * jax.random.normal(next(ks), shape, f32)

    L = DEPTH
    x = jax.random.normal(next(ks), (BATCH, SEQ, D_MODEL), f32)
    c = jax.random.normal(next(ks), (BATCH, D_MODEL), f32)
    positions = (jax.random.randint(next(ks), (BATCH, 1), 0, MAX_POS_OFFSET, dtype=jnp.int32)
                 + jnp.arange(SEQ, dtype=jnp.int32)[None, :])
    return {
        'x': x,
        'c': c,
        'positions': positions,
        'ada_w': dense((L, D_MODEL, 6 * D_MODEL), D_MODEL),
        'ada_b': 0.02 * jax.random.normal(next(ks), (L, 6 * D_MODEL), f32),
        'norm_mix': gain((L, D_MODEL)),
        'norm_mlp': gain((L, D_MODEL)),
        'w_in': dense((L, D_MODEL, IN_COLS), D_MODEL),
        'fox_b_f': jax.random.uniform(next(ks), (L, FOX_HEADS), f32, minval=1.0, maxval=4.0),
        'mla_q_norm': gain((L, MLA_Q_LORA)),
        'mla_w_uq': dense((L, MLA_Q_LORA, MLA_HEADS * (MLA_NOPE + MLA_ROPE)), MLA_Q_LORA),
        'mla_kv_norm': gain((L, MLA_KV_LORA)),
        'mla_w_ukv': dense((L, MLA_KV_LORA, MLA_HEADS * (MLA_NOPE + MLA_V)), MLA_KV_LORA),
        'nsa_pos_k': 0.1 * jax.random.normal(next(ks), (L, NSA_CMP_LEN, HEAD_DIM), f32),
        'nsa_pos_v': 0.1 * jax.random.normal(next(ks), (L, NSA_CMP_LEN, HEAD_DIM), f32),
        'nsa_cmp_k_w1': dense((L, NSA_CMP_LEN * HEAD_DIM, NSA_CMP_HIDDEN), NSA_CMP_LEN * HEAD_DIM),
        'nsa_cmp_k_w2': dense((L, NSA_CMP_HIDDEN, HEAD_DIM), NSA_CMP_HIDDEN),
        'nsa_cmp_v_w1': dense((L, NSA_CMP_LEN * HEAD_DIM, NSA_CMP_HIDDEN), NSA_CMP_LEN * HEAD_DIM),
        'nsa_cmp_v_w2': dense((L, NSA_CMP_HIDDEN, HEAD_DIM), NSA_CMP_HIDDEN),
        'out_norm': gain((L, D_MIX)),
        'w_out': dense((L, D_MIX, D_MODEL), D_MIX),
        'mlp_w1': dense((L, D_MODEL, D_FF), D_MODEL),
        'mlp_w2': dense((L, D_FF, D_MODEL), D_FF),
        'final_norm': gain((D_MODEL,)),
    }

def reference(x, c, positions, ada_w, ada_b, norm_mix, norm_mlp, w_in, fox_b_f,
              mla_q_norm, mla_w_uq, mla_kv_norm, mla_w_ukv,
              nsa_pos_k, nsa_pos_v, nsa_cmp_k_w1, nsa_cmp_k_w2, nsa_cmp_v_w1, nsa_cmp_v_w2,
              out_norm, w_out, mlp_w1, mlp_w2, final_norm):
    c_act = jax.nn.silu(c)
    for l in range(DEPTH):
        x = hybrid_layer(x, c_act, positions, ada_w[l], ada_b[l], norm_mix[l], norm_mlp[l], w_in[l], fox_b_f[l],
                         mla_q_norm[l], mla_w_uq[l], mla_kv_norm[l], mla_w_ukv[l],
                         nsa_pos_k[l], nsa_pos_v[l], nsa_cmp_k_w1[l], nsa_cmp_k_w2[l],
                         nsa_cmp_v_w1[l], nsa_cmp_v_w2[l],
                         out_norm[l], w_out[l], mlp_w1[l], mlp_w2[l])
    return rms_norm(x, final_norm)


_drawn_inputs = setup_inputs


def setup_inputs(seed=0):
    import zlib

    import numpy as np

    out = dict(_drawn_inputs(seed))
    spreads = {}
    factors = {'norm_mix': 4.883,
     'norm_mlp': 2.987,
     'mla_q_norm': 8.0,
     'mla_kv_norm': 8.0,
     'nsa_pos_k': 8.0,
     'nsa_pos_v': 2.841,
     'out_norm': 4.41,
     'final_norm': 2.807}
    for name, (base, spread) in spreads.items():
        noise = np.random.default_rng([zlib.crc32(name.encode()), seed]).standard_normal(out[name].shape)
        drawn = base * np.exp(spread * noise) if base else spread * noise
        out[name] = __import__('jax').numpy.asarray(drawn.astype(out[name].dtype))
    for name, factor in factors.items():
        out[name] = (out[name] * factor).astype(out[name].dtype)
    return out
```

```python
import numpy as np
from contextlib import ExitStack

import concourse.bass as bass
from concourse import mybir

F32 = mybir.dt.float32
F32R = mybir.dt.float32r
I32 = mybir.dt.int32
ALU = mybir.AluOpType
ACT = mybir.ActivationFunctionType
AX = mybir.AxisListType

P = 128
D = 2048
SEQ = 256
LAYERS = 2
KT = D // P
FF = 4 * D
IN_COLS = 4956
EPS = 1e-6
NEG = -1e30
MLA_SCALE = (128 + 64) ** -0.5
HEAD_SCALE = 128 ** -0.5
THETA = 500000.0
TWO_PI = 2 * np.pi

CHUNKS = [
    ("nqa", "w_in", 2368, 388, 16, 2),
    ("fq", "w_in", 832, 512, 16, 2),
    ("fk", "w_in", 1344, 512, 16, 2),
    ("fv", "w_in", 1856, 512, 16, 2),
    ("cq", "w_in", 0, 512, 16, 2),
    ("ckv", "w_in", 512, 320, 16, 2),
    ("nqb", "w_in", 2756, 512, 16, 2),
    ("uq0", "uq", 0, 384, 4, 2),
    ("kc", "w_in", 3268, 384, 16, 2),
    ("uq1", "uq", 384, 384, 4, 2),
    ("vc", "w_in", 3652, 512, 16, 2),
    ("kv0", "ukv", 0, 512, 2, 1),
    ("vs", "w_in", 4164, 512, 16, 2),
    ("kv1", "ukv", 512, 512, 2, 1),
    ("vw", "w_in", 4676, 280, 16, 2),
    ("cw1", "cw1", 0, 512, 64, 2),
    ("wo0", "w_out", 0, 512, 16, 2),
    ("wo1", "w_out", 512, 512, 16, 2),
    ("wo2", "w_out", 1024, 512, 16, 2),
    ("wo3", "w_out", 1536, 512, 16, 2),
]
CI = {c[0]: i for i, c in enumerate(CHUNKS)}
NPIECES = [c[4] // c[5] for c in CHUNKS]
FIRST = [sum(NPIECES[:i]) for i in range(len(CHUNKS))]
FRONT = sum(NPIECES)
SUPERS = 4
MLP_CHUNKS = 8
SUPER = MLP_CHUNKS * 8
PIECES = FRONT + SUPERS * SUPER
RING = 4
PCHUNKS = (len(CHUNKS) + SUPERS * MLP_CHUNKS) // 2
assert FRONT % RING == 0 and SUPER % RING == 0 and len(CHUNKS) % 2 == 0

ADA_N = 1024
ADA_FRONT = 8 * KT
ADA_LAYER = ADA_FRONT + SUPERS * KT
assert ADA_FRONT <= FRONT

UNITS = [("fox", h) for h in range(4)] + [("mla", h) for h in range(4)] + \
        [("slc", h) for h in range(8)] + [("win", h) for h in range(8)]
NU = len(UNITS)
SLOTS = [0, 1, 2, 3, None, None] + list(range(4, NU)) + [None, None]


def piece(name, p):
    return FIRST[CI[name]] + p


STEPS_PE = {}
STEPS_SIDE = {}


def pe_at(q, step):
    STEPS_PE.setdefault(q, []).append(step)


def side_at(q, step):
    STEPS_SIDE.setdefault(q, []).append(step)


def t_step(q, name, lag=2):
    pe_at(q, ("T", name))
    side_at(q + lag, ("T", name))


for host, done in (("fq", "nqa"), ("fk", "fq"), ("fv", "fk"), ("cq", "fv"), ("ckv", "cq"), ("nqb", "ckv"),
                   ("uq0", "nqb"), ("kc", "uq0"), ("uq1", "kc"), ("vc", "uq1"), ("kv0", "vc"), ("vs", "kv0"),
                   ("kv1", "vs"), ("vw", "kv1"), ("cw1", "vw"), ("wo1", "wo0"), ("wo2", "wo1"), ("wo3", "wo2")):
    side_at(piece(host, 1), ("evac", done))
for q, name in ((piece("fq", 2), "nqa0"), (piece("fq", 4), "nqa1"), (piece("fq", 6), "cum"),
                (piece("fk", 2), "fq0"), (piece("fk", 4), "fq1"), (piece("fv", 2), "fk0"), (piece("fv", 4), "fk1"),
                (piece("ckv", 3), "cq0"), (piece("ckv", 5), "cq1"), (piece("nqb", 3), "ckv0"),
                (piece("nqb", 5), "kr"), (piece("kc", 0), "nqb0"), (piece("kc", 2), "nqb1"),
                (piece("kc", 4), "uq0n"), (piece("kc", 6), "uq0r"), (piece("vc", 0), "nq7"),
                (piece("vc", 2), "kcT"), (piece("vc", 4), "uq1n"), (piece("vc", 6), "uq1r"),
                (piece("vs", 0), "vcT"), (piece("vs", 2), "ks"), (piece("vs", 4), "k0"),
                (piece("vw", 0), "kw"), (piece("vw", 2), "k1"),
                (piece("cw1", 5), "ofox0"), (piece("cw1", 7), "ofox1"),
                (piece("cw1", 11), "omla0"), (piece("cw1", 13), "omla1"),
                (piece("cw1", 18), "hid0"), (piece("cw1", 21), "kcmp"), (piece("cw1", 23), "csc"),
                (piece("cw1", 26), "cpt")):
    t_step(q, name)
side_at(piece("cw1", 3), ("rms", "ofox"))
side_at(piece("cw1", 9), ("rms", "omla"))
side_at(piece("cw1", 17), ("hpre", 0))
for b in range(8):
    t_step(16 * b + 14, f"ada{b}")
for s, q in enumerate([piece("ckv", 0), piece("ckv", 2), piece("ckv", 4), piece("ckv", 6), piece("nqb", 0),
                       piece("nqb", 2), piece("vw", 4), piece("vw", 6)]
                      + [piece("cw1", 0) + (3 * k) // 2 for k in range(20)]):
    pe_at(q, ("slot", s))
    side_at(q + 2, ("slot", s))
assert len(SLOTS) == 28
W = piece("wo0", 0)
side_at(W + 1, ("hpre", 1))
for name in ("hid1", "vcmp", "vrep", "co0", "co1", "co2", "co3"):
    t_step(W + 3, name)
side_at(W + 5, ("rms", "onsa"))
for name in ("onsa0", "onsa1", "onsa2", "onsa3"):
    t_step(W + 3, name)
side_at(W + 5, ("diag", 0))
side_at(W + 5, ("diag", 1))
for j in range(4):
    t_step(W + 4 + j, f"gta{j}", lag=3)
    t_step(W + 10 + 2 * j, f"gtm{j}")
GATE_ROWS = [f"gta{j}" for j in range(4)] + [f"gtm{j}" for j in range(4)]

CHUNK_OF = [i for i in range(len(CHUNKS)) for p in range(NPIECES[i])]
N1_PIECES = {f"n1_{k}": [k + 2] for k in range(2, 8)}
N1_PIECES["n1_0"], N1_PIECES["n1_1"] = [], list(range(4))

N1T = [f"n1_{k}" for k in range(8)]
N2T = [f"n2_{k}" for k in range(8)]
T_NAMES = N1T + [s[1] for q in range(FRONT) for s in STEPS_PE.get(q, []) if s[0] == "T"] + N2T
T_NO = {n: i for i, n in enumerate(T_NAMES)}
T_FRONT = len(T_NAMES)
T_SUPER = 9
T_LAYER = T_FRONT + SUPERS * T_SUPER
T_PROLOGUE = 4 + 4
PACKS = 4

Y_NAMES = [f"n1y{j}" for j in range(4)] + ["nqa", "fq", "fk", "cq", "ckv", "nqb", "uq0", "kc", "uq1", "vc",
                                           "kv0", "vs", "kv1"] + [f"n2y{j}" for j in range(4)]
Y_NO = {n: i for i, n in enumerate(Y_NAMES)}
Y_FRONT = len(Y_NAMES)
Y_LAYER = Y_FRONT + SUPERS * 4
Y_LAST_T = {"nqa": "nqa1", "fq": "fq1", "fk": "fk1", "cq": "cq1", "ckv": "kr", "nqb": "nqb1", "uq0": "uq0r",
            "kc": "kcT", "uq1": "uq1r", "vc": "ks", "kv0": "k0", "vs": "kw", "kv1": "k1"}
for j in range(4):
    Y_LAST_T[f"n1y{j}"] = f"n1_{2 * j + 1}"
    Y_LAST_T[f"n2y{j}"] = f"n2_{2 * j + 1}"
Y_LAST_SPLIT = {"cq": "cq1", "ckv": "ckv0"}
for j in range(4):
    Y_LAST_SPLIT[f"n1y{j}"] = f"n1_{2 * j + 1}"
    Y_LAST_SPLIT[f"n2y{j}"] = f"n2_{2 * j + 1}"
SPLIT_NAMES = [n for n in T_NAMES if n[:2] in ("n1", "n2") or n in
               ("cq0", "cq1", "ckv0", "kcT", "vcT", "ofox0", "ofox1", "omla0", "omla1",
                "onsa0", "onsa1", "onsa2", "onsa3")]
SPLIT_NO = {n: i for i, n in enumerate(SPLIT_NAMES)}
SPLIT_FRONT = len(SPLIT_NAMES)
SPLIT_LAYER = SPLIT_FRONT + SUPERS * 8
RMS_NAMES = ["n1", "cq", "ckv", "ofox", "omla", "onsa", "n2"]
RMS_NO = {n: i for i, n in enumerate(RMS_NAMES)}
RMS_LAYER = len(RMS_NAMES)

GAINS = 54
G_MIX, G_MLP, G_OUT, G_Q, G_KV = 0, 16, 32, 48, 52

DVE_PROLOGUE, DVE_FRONT, DVE_SUPER = 30, 260, 20


def trunk(nc, x, c, positions, inv_freq, ada_w, ada_b, norm_mix, norm_mlp, w_in, fox_b_f, mla_q_norm, mla_w_uq,
          mla_kv_norm, mla_w_ukv, nsa_pos_k, nsa_pos_v, cmp_k_w1, cmp_k_w2, cmp_v_w1, cmp_v_w2,
          out_norm, w_out, mlp_w1, mlp_w2, final_norm, out):
    with ExitStack() as ctx:
        def sb(name, shape, dt=F32):
            return ctx.enter_context(nc.sbuf_tensor(name, shape, dt))

        def sem(name):
            return ctx.enter_context(nc.semaphore(name))

        X = sb("X", [P, 2, D])
        hT_hi, hT_lo = sb("hT_hi", [P, KT, SEQ], F32R), sb("hT_lo", [P, KT, SEQ], F32R)
        uT_hi, uT_lo = sb("uT_hi", [P, KT, SEQ], F32R), sb("uT_lo", [P, KT, SEQ], F32R)
        w_raw = sb("w_raw", [P, RING, 2, 512])
        w_hi, w_lo = sb("w_hi", [P, RING, 2, 512], F32R), sb("w_lo", [P, RING, 2, 512], F32R)
        ada_raw = sb("ada_raw", [P, 2, ADA_N])
        ada_acc = sb("ada_acc", [P, ADA_N])
        ybuf = sb("ybuf", [P, 2, 2, 512])
        arena = sb("arena", [P, 12544])
        ident, ones, tri, causal = sb("ident", [P, P]), sb("ones", [P, P]), sb("tri", [P, P]), sb("causal", [P, P])
        gcols = sb("gcols", [P, LAYERS * GAINS + KT])
        bcols = sb("bcols", [P, LAYERS, 96])
        posT = sb("posT", [P, LAYERS, 2, 32])
        g = sb("g", [P, GAINS])
        ada_A = sb("ada_A", [P, 32])
        ada_B = sb("ada_B", [P, 64])
        mscale = sb("mscale", [P, KT])
        silu_c = sb("silu_c", [P, KT])
        bcur = sb("bcur", [P, 64])
        pos_l = sb("pos_l", [P, 2, 32])
        cos, sin = sb("cos", [P, 2, 32]), sb("sin", [P, 2, 32])
        rope_a, rope_b = sb("rope_a", [P, P]), sb("rope_b", [P, P])
        fbias = sb("fbias", [P, LAYERS, 4])
        cmask = sb("cmask", [P, 2, 16])
        any_ok = sb("any_ok", [P, 2])
        Rsel = sb("Rsel", [32, P])
        I2 = sb("I2", [64, 32])
        bmask = sb("bmask", [P, 8])
        small = sb("small", [P, 160])
        ss, ms, rstd, mhalf = small[:, 0:2], small[:, 2:4], small[:, 4:6], small[:, 6:8]
        pos_f = small[:, 8:10]
        nmax = small[:, 16:24].rearrange("p (u b) -> p u b", u=4)
        psums = small[:, 24:32].rearrange("p (u b) -> p u b", u=4)
        fac = small[:, 32:34]
        lf = small[:, 40:48].rearrange("p (m h) -> p m h", m=2)
        lfa = small[:, 48:56].rearrange("p (m h) -> p m h", m=2)
        lfb = small[:, 56:64].rearrange("p (m h) -> p m h", m=2)
        gates = small[:, 64:112].rearrange("p (m h r) -> p m h r", m=2, h=8)
        cmx, csum = small[:, 112:128], small[:, 128:144]

        def area(at, n):
            return arena[:, at:at + n]

        FQ = area(0, 1024).rearrange("p (h t) -> p h t", h=4)
        FK = area(1024, 1024).rearrange("p (h t) -> p h t", h=4)
        FV = area(2048, 1024).rearrange("p (m n) -> p m n", m=2)
        KS = area(1024, 512).rearrange("p (g t) -> p g t", g=2)
        KW = area(1536, 512).rearrange("p (g t) -> p g t", g=2)
        VS = area(2048, 512).rearrange("p (m n) -> p m n", m=2)
        VW = area(2560, 512).rearrange("p (m n) -> p m n", m=2)
        MQ = area(3072, 1024).rearrange("p (h t) -> p h t", h=4)
        MQR = area(4096, 512).rearrange("p (a t) -> p a t", a=2)
        MKR = area(4608, 256)
        MK = area(4864, 1024).rearrange("p (h t) -> p h t", h=4)
        MV = area(5888, 1024).rearrange("p (m n) -> p m n", m=2)
        NQ = area(6912, 2048).rearrange("p (h t) -> p h t", h=8)
        ONSA = area(8960, 2048).rearrange("p (h m n) -> p h m n", h=8, m=2)
        Pb = area(11008, 768).rearrange("p (u n) -> p u n", u=2)
        PTb = area(11776, 768).rearrange("p (u n) -> p u n", u=2)
        cum, ncum = arena[0:4, 4864:5120], arena[0:4, 5120:5376]
        junk = area(8960, 1024)
        blk = area(8960, 1024).rearrange("p (l r) -> p l r", l=32)
        hpre = arena[0:64, 4096:4608]
        hid = area(0, 128).rearrange("p (j r) -> p j r", j=4)
        hx, ht = area(128, 128), area(256, 128)
        cs = area(384, 256)
        cpt = area(640, 256).rearrange("p (m q) -> p m q", m=2)
        kcmp = area(896, 32)
        vcmp = arena[0:32, 3072:3200]
        cw2 = [area(5888, 512).rearrange("p (j n) -> p j n", j=4), area(6400, 512).rearrange("p (j n) -> p j n", j=4)]
        VBD = area(4864, 1024).rearrange("p (h n) -> p h n", h=8)
        GTA = area(6912, 2048)
        GTM = area(1024, 2048)
        FNB = area(6912, 2048)
        O_FOX = area(0, 1024).rearrange("p (h m n) -> p h m n", h=4, m=2)
        O_MLA = area(3072, 1024).rearrange("p (h m n) -> p h m n", h=4, m=2)
        uflat_hi = uT_hi[:, :, :].rearrange("p k t -> p (k t)")
        uflat_lo = uT_lo[:, :, :].rearrange("p k t -> p (k t)")
        BLK = [uflat_hi[:, 1536:1536 + 33 * 64], uflat_lo[:, 1536:1536 + 33 * 64]]
        diag = ybuf[:, :, :, :].rearrange("p b m n -> p (b m) n")
        junk_y = ybuf[:, :, :, :].rearrange("p b m n -> p (b m n)")

        acc = [ctx.enter_context(nc.psum_tensor(f"acc{i}", [P, 2, 512], F32)) for i in range(2)]
        bank_S = ctx.enter_context(nc.psum_tensor("bank_S", [P, 4, P], F32))
        bank_PT = ctx.enter_context(nc.psum_tensor("bank_PT", [P, 4, P], F32))
        bank_O = ctx.enter_context(nc.psum_tensor("bank_O", [P, 2, SEQ], F32))
        bank_T = ctx.enter_context(nc.psum_tensor("bank_T", [P, 2, SEQ], F32))
        T512 = bank_T[:, :, :].rearrange("p a t -> p (a t)")

        loaded = sem("loaded")
        packed = sem("packed")
        consts = sem("consts")
        raw_landed = [sem(f"raw_landed{i}") for i in range(RING)]
        hi_done, lo_done, piece_used = sem("hi_done"), sem("lo_done"), sem("piece_used")
        acc_free = [sem("acc_free0"), sem("acc_free1")]
        ada_landed = [sem("ada_landed0"), sem("ada_landed1")]
        ada_used = sem("ada_used")
        t_full, t_free = sem("t_full"), sem("t_free")
        y_full = sem("y_full")
        v_hi, split_done = sem("v_hi"), sem("split_done")
        x_landed, out_ready = sem("x_landed"), sem("out_ready")
        sumsq, meansq, rstd_done = sem("sumsq"), sem("meansq"), sem("rstd_done")
        rms_src = sem("rms_src")
        s_scores, s_max, s_exp = sem("s_scores"), sem("s_max"), sem("s_exp")
        s_pt, s_ptev, s_pv, s_oev = sem("s_pt"), sem("s_ptev"), sem("s_pv"), sem("s_oev")
        fz, fe, fl = sem("fz"), sem("fe"), sem("fl")
        gate_in, gate_e = sem("gate_in"), sem("gate_e")
        gelu_in, gelu_t, hid_done = sem("gelu_in"), sem("gelu_t"), sem("hid_done")
        hpre_done = sem("hpre_done")
        cmp_x, cmp_e, cmp_p = sem("cmp_x"), sem("cmp_e"), sem("cmp_p")
        cw2_landed = sem("cw2_landed")
        fn_landed = sem("fn_landed")
        diag_done = sem("diag_done")
        o_ready = sem("o_ready")
        dve_own, pool_own = sem("dve_own"), sem("pool_own")
        stored = sem("stored")
        silu_e, ang_ready, trig_done = sem("silu_e"), sem("ang_ready"), sem("trig_done")

        w_dram = {"w_in": (w_in.rearrange("l k n -> (l k) n"), D), "uq": (mla_w_uq.rearrange("l k n -> (l k) n"), 512),
                  "ukv": (mla_w_ukv.rearrange("l k n -> (l k) n"), 256),
                  "w_out": (w_out.rearrange("l k n -> (l k) n"), D)}
        cw1_dram = [cmp_k_w1.rearrange("l k n -> (l k) n"), cmp_v_w1.rearrange("l k n -> (l k) n")]
        cw2_dram = [cmp_k_w2.rearrange("l k n -> (l k) n"), cmp_v_w2.rearrange("l k n -> (l k) n")]
        w1_dram = mlp_w1.rearrange("l k n -> (l k) n")
        w2_dram = mlp_w2.rearrange("l k n -> (l k) n")
        ada_dram = ada_w.rearrange("l k n -> (l k) n")
        x_dram = x.rearrange("a (m p) d -> p (a m) d", p=P)
        out_dram = out.rearrange("a (m p) d -> p (a m) d", p=P)

        def layer_t(l, n):
            return l * T_LAYER + T_PROLOGUE + n + 1

        def used(l, q):
            return l * PIECES + q + 1 + RING

        def chunk_done(l, name):
            return used(l, FIRST[CI[name]] + NPIECES[CI[name]] - 1)

        def y_slot(n):
            return ybuf[:, n % 2]

        def v_half(n, t):
            return ybuf[:, n % 2, :, 256 * t:256 * t + 256]

        block = ctx.enter_context(nc.Block())

        @block.sync
        def _(sp):
            rows = diag[:, :, 0:P]
            for l in range(LAYERS):
                o = l * GAINS
                for v, at, n in ((norm_mix, G_MIX, 16), (norm_mlp, G_MLP, 16), (out_norm, G_OUT, 16),
                                 (mla_q_norm, G_Q, 4), (mla_kv_norm, G_KV, 2)):
                    sp.dma_start(rows[o + at:o + at + n, 0, :], v[l].rearrange("(k p) -> k p", p=P)).then_inc(packed, 16)
                sp.dma_start(rows[0:96, 1 + l, :], ada_b[l].rearrange("(k p) -> k p", p=P)).then_inc(packed, 16)
                sp.dma_start(rows[64 * l:64 * l + 32, 3, :], nsa_pos_k[l]).then_inc(packed, 16)
                sp.dma_start(rows[64 * l + 32:64 * l + 64, 3, :], nsa_pos_v[l]).then_inc(packed, 16)
            o = LAYERS * GAINS
            sp.dma_start(rows[o:o + KT, 0, :], c[0].rearrange("(k p) -> k p", p=P)).then_inc(packed, 16)

            sp.dma_start(rope_b[:, 0:2].bitcast(I32), positions.rearrange("a (m p) -> p (a m)", p=P),
                         allow_slow_non_contiguous=True
                         ).then_inc(loaded, 16)
            sp.dma_start(rope_b[:, 32:64], inv_freq.broadcast_to([P, 32])).then_inc(loaded, 16)
            sp.dma_start(fbias[:, :, :].rearrange("p l h -> p (l h)"),
                         fox_b_f.rearrange("(a l) h -> a (l h)", a=1).broadcast_to([P, LAYERS * 4])).then_inc(loaded, 16)
            sp.dma_start(X[:, :, :], x_dram).then_inc(x_landed, 16)

            def ada_tile(at, first_row, col, n):
                row, col = sp.snap(first_row), sp.snap(col)
                sp.wait_ge(ada_used, at + n + 1)
                sp.dma_start(ada_raw[:, n % 2, :], ada_dram[bass.ds(row, P), bass.ds(col, ADA_N)]
                             ).then_inc(ada_landed[n % 2], 16)

            with sp.Fori(0, SUPERS) as b:
                for kt in range(KT):
                    ada_tile(b * KT, kt * P, b * ADA_N, kt)

            def put(at, q, weights, row, nk, col, n):
                if type(col) is int:
                    width = weights.shape[1]
                    start = sp.snap(row * width)
                    src = weights.rearrange("k n -> (k n)")[bass.ds(start, nk * P * width)]
                    src = src.rearrange("(k n) -> k n", n=width)[:, col:col + n]
                else:
                    row, col = sp.snap(row), sp.snap(col)
                    src = weights[bass.ds(row, nk * P), bass.ds(col, n)]
                sp.wait_ge(lo_done, at + q + 1)
                sp.dma_start(w_raw[:, q % RING, 0:nk, 0:n], src.rearrange("(k p) n -> p k n", p=P)
                             ).then_inc(raw_landed[q % RING], 16)

            with sp.Fori(0, LAYERS) as l:
                for i, (name, w, c0, n, kts, per) in enumerate(CHUNKS):
                    for p in range(NPIECES[i]):
                        q = FIRST[i] + p
                        if w == "cw1":
                            put(l * PIECES, q, cw1_dram[p // 16], l * 4096 + (p % 16) * 256, 2, 0, 512)
                        else:
                            weights, k = w_dram[w]
                            row = (l + 1) * k + (p * per * P - k) if name == "cq" else l * k + p * per * P
                            put(l * PIECES, q, weights, row, per, c0, n)
                        n_ada = q - 2
                        if 0 <= n_ada < ADA_FRONT:
                            ada_tile(l * ADA_LAYER + SUPERS * KT, l * D + (n_ada % KT) * P, 4096 + (n_ada // KT) * ADA_N,
                                     n_ada)
                        if q == piece("cw1", 18):
                            sp.wait_ge(s_oev, l * NU + 8)
                            for j in range(2):
                                sp.dma_start(cw2[j], cw2_dram[j][bass.ds(l * 512, 512), :]
                                             .rearrange("(k p) n -> p k n", p=P)).then_inc(cw2_landed, 16)
                with sp.Fori(0, SUPERS) as s:
                    for ch in range(MLP_CHUNKS):
                        for p in range(8):
                            q = ch * 8 + p
                            at = l * PIECES + FRONT + s * SUPER
                            if ch < 4:
                                put(at, q, w1_dram, l * D + p * 256, 2, s * D + ch * 512, 512)
                            else:
                                put(at, q, w2_dram, l * FF + s * D + p * 256, 2, (ch - 4) * 512, 512)
                            if q % 4 == 1:
                                ada_tile(l * ADA_LAYER + SUPERS * KT + ADA_FRONT + s * KT,
                                         l * -D + D + (q // 4) * P, s * ADA_N, q // 4)
            sp.wait_ge(sumsq, 2 * LAYERS * RMS_LAYER)
            sp.dma_start(FNB, final_norm.rearrange("(a n) -> a n", a=1).broadcast_to([P, D])).then_inc(fn_landed, 16)
            sp.wait_ge(out_ready, 1)
            sp.dma_start(out_dram, X[:, :, :]).then_inc(stored, 16)
            sp.wait_ge(stored, 16)

        @block.gpsimd
        def _(pool):
            n = 0
            gp = nc.gpsimd

            def link(ins):
                nonlocal n
                n += 1
                ins.then_inc(pool_own, 1)
                pool.wait_ge(pool_own, n)

            def select(out_, fill, base, pattern, mult, op=ALU.is_ge):
                link(gp.affine_select(out=out_, in_=out_, compare_op=op, fill=fill, base=base, pattern=pattern,
                                      channel_multiplier=mult))

            link(gp.memset(ident[:], 0.0))
            select(ident[:], 1.0, 0, [[-1, P]], 1, ALU.not_equal)
            link(gp.memset(ones[:], 1.0))
            link(gp.memset(mhalf, -0.5))
            link(gp.memset(tri[:], 1.0))
            select(tri[:], 0.0, 0, [[1, P]], -1)
            link(gp.memset(causal[:], 0.0))
            select(causal[:], NEG, 0, [[-1, P]], 1)
            link(gp.memset(cmask[:], 0.0))
            select(cmask[:], NEG, -31, [[P, 2], [-16, 16]], 1)
            link(gp.memset(cmask[:, :, 15:16], NEG))
            link(gp.memset(any_ok[:], 1.0))
            select(any_ok[:], 0.0, -31, [[P, 2]], 1)
            link(gp.memset(bmask[:], 1.0))
            select(bmask[:], 0.0, 0, [[-16, 8]], 1)
            select(bmask[:], 0.0, 15, [[16, 8]], -1)
            link(gp.memset(Rsel[:], 0.0))
            r4 = Rsel[:].rearrange("r (g h n) -> r g h n", g=2, h=4)
            select(r4, 1.0, 0, [[-16, 2], [0, 4], [-1, 16]], 1, ALU.not_equal)
            link(gp.memset(I2[:], 0.0))
            select(I2[:], 1.0, 0, [[-1, 32]], 1, ALU.not_equal)
            select(I2[:], 1.0, -32, [[-1, 32]], 1, ALU.not_equal)
            link(gp.memset(uT_hi[:, 6:16, :].bitcast(F32), 0.0))
            gp.memset(uT_lo[:, 6:16, :].bitcast(F32), 0.0).then_inc(consts, 1)
            with pool.Fori(0, RMS_LAYER * LAYERS + 1) as r:
                pool.wait_ge(meansq, r + 1)
                gp.tensor_tensor(rstd, ms, mhalf, ALU.pow).then_inc(rstd_done, 1)

        @block.scalar
        def _(act):
            a = nc.scalar

            act.wait_ge(t_free, 1)
            a.activation(silu_c[:], gcols[:, LAYERS * GAINS:], ACT.Exp, scale=-1.0).then_inc(silu_e, 1)
            act.wait_ge(ang_ready, 1)
            a.activation(cos[:], cos[:], ACT.Sin)
            a.activation(sin[:], sin[:], ACT.Sin).then_inc(trig_done, 1)

            def hi(at, q, nk, n):
                act.wait_ge(raw_landed[q % RING], landed_value(at, q))
                act.wait_ge(piece_used, at[0] * PIECES + at[1] * SUPER + at[2] + q + 1)
                a.activation(w_hi[:, q % RING, 0:nk, 0:n], w_raw[:, q % RING, 0:nk, 0:n], ACT.Copy).then_inc(hi_done, 1)

            def landed_value(at, q):
                return 16 * (at[0] * (PIECES // RING) + at[1] * (SUPER // RING) + at[2] // RING + q // RING + 1)

            def square_sum(l, name, srcs, junks):
                r = l * RMS_LAYER + (RMS_NO[name] if name != "final" else 0)
                for m in range(2):
                    if m:
                        act.wait_ge(sumsq, 2 * r + 1)
                    a.activation(junks[m], srcs[m], ACT.Square, accum_out=ss[:, m:m + 1]).then_inc(sumsq, 1)

            def split_hi(l, name, v, dst):
                act.wait_ge(t_free, layer_t(l, T_NO[name]))
                a.activation(dst, v, ACT.Copy).then_inc(v_hi, 1)

            def turn_out(l, name, dst, n, scale=1.0):
                act.wait_ge(t_full, layer_t(l, T_NO[name]))
                a.activation(dst, T512[:, 0:n], ACT.Copy, scale=scale).then_inc(t_free, 1)

            def flat(ap):
                return ap.rearrange("p a t -> p (a t)")

            def t_out(l, name):
                if name in ("nqa0", "nqa1", "nqb0", "nqb1", "nq7"):
                    h0, n = {"nqa0": (0, 2), "nqa1": (2, 1), "nqb0": (3, 2), "nqb1": (5, 2), "nq7": (7, 1)}[name]
                    turn_out(l, name, flat(NQ[:, h0:h0 + n, :]), n * SEQ, HEAD_SCALE)
                elif name in ("fq0", "fq1"):
                    j = int(name[-1])
                    turn_out(l, name, flat(FQ[:, 2 * j:2 * j + 2, :]), 512, HEAD_SCALE)
                elif name in ("fk0", "fk1"):
                    j = int(name[-1])
                    turn_out(l, name, flat(FK[:, 2 * j:2 * j + 2, :]), 512)
                elif name in ("uq0n", "uq1n"):
                    j = int(name[2])
                    turn_out(l, name, flat(MQ[:, 2 * j:2 * j + 2, :]), 512, MLA_SCALE)
                elif name in ("uq0r", "uq1r"):
                    turn_out(l, name, MQR[:, int(name[2]), :], SEQ, MLA_SCALE)
                elif name in ("k0", "k1"):
                    j = int(name[-1])
                    turn_out(l, name, flat(MK[:, 2 * j:2 * j + 2, :]), 512)
                elif name == "kr":
                    turn_out(l, name, MKR, SEQ)
                elif name == "ks":
                    turn_out(l, name, flat(KS), 512)
                elif name == "kw":
                    turn_out(l, name, flat(KW), 512)
                elif name in ("cq0", "cq1"):
                    j = int(name[-1])
                    split_hi(l, name, v_half(Y_NO["cq"], j), uT_hi[:, 2 * j:2 * j + 2, :])
                elif name == "ckv0":
                    split_hi(l, name, v_half(Y_NO["ckv"], 0), uT_hi[:, 4:6, :])
                elif name in ("kcT", "vcT"):
                    j = ("kcT", "vcT").index(name)
                    split_hi(l, name, blk, BLK[j][:, 0:2048].rearrange("p (l r) -> p l r", l=32)[:, :, 0:32])
                elif name in ("ofox0", "ofox1"):
                    j = int(name[-1])
                    split_hi(l, name, FQ[:, 2 * j:2 * j + 2, :], hT_hi[:, 4 + 2 * j:6 + 2 * j, :])
                elif name in ("omla0", "omla1"):
                    j = int(name[-1])
                    split_hi(l, name, MQ[:, 2 * j:2 * j + 2, :], hT_hi[:, 2 * j:2 * j + 2, :])
                elif name.startswith("onsa"):
                    j = int(name[-1])
                    split_hi(l, name, ONSA_T[:, 2 * j:2 * j + 2, :], hT_hi[:, 8 + 2 * j:10 + 2 * j, :])
                elif name.startswith("n1_") or name.startswith("n2_"):
                    k = int(name[3:])
                    split_hi(l, name, v_half(Y_NO[name[0:2] + "y0"] + k // 2, k % 2), hT_hi[:, 2 * k:2 * k + 2, :])
                elif name in ("hid0", "hid1"):
                    j = int(name[-1])
                    act.wait_ge(gelu_in, l * 2 + j + 1)
                    a.activation(ht, ht, ACT.Tanh, scale=float(np.sqrt(2 / np.pi))).then_inc(gelu_t, 1)
                elif name == "csc":
                    act.wait_ge(cmp_x, l + 1)
                    a.activation(cs, cs, ACT.Exp).then_inc(cmp_e, 1)
                elif name == "cpt":
                    turn_out(l, name, flat(cpt), 256)
                elif name[:3] in ("gta", "gtm"):
                    j = int(name[-1])
                    dst = GTA if name[:3] == "gta" else GTM
                    act.wait_ge(t_full, layer_t(l, T_NO[name]))
                    a.activation(dst[:, 512 * j:512 * j + 512], T512, ACT.Copy).then_inc(t_free, 1)

            def slot(l, s):
                u = SLOTS[s]
                b = SLOTS[s - 1] if s >= 1 else None
                if b is not None:
                    act.wait_ge(s_pt, l * NU + b + 1)
                    a.activation(PTb[:, b % 2, :], bank_PT[:, 0:3, :].rearrange("p a t -> p (a t)"), ACT.Copy
                                 ).then_inc(s_ptev, 1)
                if u is not None:
                    act.wait_ge(s_max, l * NU + u + 1)
                    a.activation(Pb[:, u % 2, 0:128], bank_S[:, 0, :], ACT.Exp, bias=nmax[:, u % 4, 0:1],
                                 accum_out=psums[:, u % 4, 0:1])
                    a.activation(Pb[:, u % 2, 128:384], bank_S[:, 1:3, :].rearrange("p a t -> p (a t)"), ACT.Exp,
                                 bias=nmax[:, u % 4, 1:2], accum_out=psums[:, u % 4, 1:2]).then_inc(s_exp, 1)

            ONSA_T = area(8960, 2048).rearrange("p (h t) -> p h t", h=8)

            def rms(l, name):
                act.wait_ge(rms_src, l * RMS_LAYER + RMS_NO[name] + 1)
                if name in ("n1", "n2"):
                    srcs, junks = [X[:, m, :] for m in range(2)], [junk_y] * 2
                elif name == "cq":
                    srcs, junks = [y_slot(Y_NO["cq"])[:, m, 0:512] for m in range(2)], [junk[:, 0:512]] * 2
                elif name == "ckv":
                    srcs, junks = [y_slot(Y_NO["ckv"])[:, m, 0:256] for m in range(2)], [junk[:, 0:256]] * 2
                elif name == "onsa":
                    srcs = [ONSA[:, :, m, :] for m in range(2)]
                    junks = [junk_y[:, 0:1024].rearrange("p (h n) -> p h n", h=8)] * 2
                else:
                    o = O_FOX if name == "ofox" else O_MLA
                    srcs = [o[:, :, m, :] for m in range(2)]
                    junks = [junk_y[:, 0:512].rearrange("p (h n) -> p h n", h=4)] * 2
                square_sum(l, name, srcs, junks)

            def side_piece(l, q):
                i = CHUNK_OF[q]
                hi((l, 0, 0), q, CHUNKS[i][5], CHUNKS[i][3])
                for kind, what in STEPS_SIDE.get(q, []):
                    if kind == "T":
                        t_out(l, what)
                    elif kind == "slot":
                        slot(l, what)
                    elif kind == "rms":
                        rms(l, what)
                    elif kind == "evac" and what in ("cq", "ckv"):
                        rms(l, what)
                    elif kind == "evac" and what == "nqa":
                        act.wait_ge(fz, l + 1)
                        a.activation(lfb, lfb, ACT.Exp, scale=-1.0).then_inc(fe, 1)
                        act.wait_ge(fe, 2 * l + 1)
                        a.activation(lfb, lfb, ACT.Ln, bias=1.0).then_inc(fe, 1)
                    elif kind == "evac" and what == "vw":
                        act.wait_ge(gate_in, l + 1)
                        a.activation(gates[:, :, :, :], gates[:, :, :, :], ACT.Exp, scale=-1.0).then_inc(gate_e, 1)
                    elif kind == "hpre":
                        act.wait_ge(piece_used, used(l, piece("cw1", 15 + 16 * what)))
                        if what:
                            act.wait_ge(t_full, layer_t(l, T_NO["hid0"]))
                        a.activation(hpre, acc[CI["cw1"] % 2][0:64, what, :], ACT.Copy
                                     ).then_inc(acc_free[CI["cw1"] % 2] if what else hpre_done, 1)

            with act.Fori(0, LAYERS) as l:
                rms(l, "n1")
                for n in N1T:
                    t_out(l, n)
                    for q in N1_PIECES[n]:
                        side_piece(l, q)
                for q in range(N1_PIECES[N1T[-1]][-1] + 1, FRONT):
                    side_piece(l, q)
                rms(l, "n2")
                for n in N2T:
                    t_out(l, n)
                with act.Fori(0, SUPERS) as s:
                    at = (l, s, FRONT)
                    for ch in range(MLP_CHUNKS):
                        for p in range(8):
                            q = ch * 8 + p
                            hi(at, q, 2, 512)
                            j = ch - 1
                            if 0 <= j < 4:
                                ydone = l * Y_LAYER + Y_FRONT + s * 4 + j
                                splits = l * SPLIT_LAYER + SPLIT_FRONT + s * 8
                                tdone = l * T_LAYER + T_PROLOGUE + T_FRONT + s * T_SUPER + 2 * j
                                if p == 1:
                                    act.wait_ge(piece_used, l * PIECES + s * SUPER + FRONT + 8 * ch + RING)
                                    if j == 0:
                                        act.wait_ge(acc_free[1], l * PCHUNKS + s * 4 + len(CHUNKS) // 2 + 1)
                                    if j >= 2:
                                        act.wait_ge(split_done, splits + 2 * (j - 1))
                                    a.activation(y_slot(j)[:, :, :], acc[j % 2][:, :, :], ACT.Relu).then_inc(y_full, 1)
                                    act.wait_ge(y_full, ydone + 1)
                                    act.sem_inc(acc_free[j % 2], 1)
                                if p in (3, 5):
                                    t = (p - 3) // 2
                                    act.wait_ge(t_full, tdone + t + 1)
                                    a.activation(v_half(j, t), bank_T[:, :, :], ACT.Square).then_inc(t_free, 1)
                                    act.wait_ge(t_free, tdone + t + 1)
                                    kt = 4 * j + 2 * t
                                    a.activation(uT_hi[:, kt:kt + 2, :], v_half(j, t), ACT.Copy).then_inc(v_hi, 1)
            act.wait_ge(rms_src, LAYERS * RMS_LAYER + 1)
            square_sum(LAYERS, "final", [X[:, m, :] for m in range(2)], [junk_y] * 2)

        @block.vector
        def _(dve):
            v = nc.vector
            own = [0, 0]

            def link(ins):
                own[0] += 1
                ins.then_inc(dve_own, 1)
                dve.wait_ge(dve_own, own[1] + own[0])

            def region(base, count):
                own[0], own[1] = 0, base
                return count

            def close(count):
                assert own[0] <= count, own
                if count > own[0]:
                    dve.sem_inc(dve_own, count - own[0])

            def bc(ap, axis, n):
                ap = ap.unsqueeze(axis)
                shape = list(ap.shape)
                shape[axis] = n
                return ap.broadcast_to(shape)

            count = region(0, DVE_PROLOGUE)
            dve.sem_inc(lo_done, RING)
            dve.sem_inc(ada_used, 2)
            dve.wait_ge(t_full, 1)
            v.tensor_copy(gcols[:], T512[:, 0:LAYERS * GAINS + KT]).then_inc(t_free, 1)
            for l in range(LAYERS):
                dve.wait_ge(t_full, 2 + l)
                v.tensor_copy(bcols[:, l, :], T512[:, 0:96]).then_inc(t_free, 1)
            dve.wait_ge(t_full, 4)
            v.tensor_copy(posT[:].rearrange("p l k s -> p (l k s)"), T512[:, 0:P]).then_inc(t_free, 1)
            dve.wait_ge(silu_e, 1)
            link(v.tensor_scalar_add(silu_c[:], silu_c[:], 1.0))
            link(v.reciprocal(silu_c[:], silu_c[:]))
            dve.wait_ge(t_free, 1)
            link(v.tensor_tensor(silu_c[:], silu_c[:], gcols[:, LAYERS * GAINS:], ALU.mult))
            dve.wait_ge(loaded, 48)
            pos_i = rope_b[:, 0:2].bitcast(I32)
            freq = rope_b[:, 32:64]
            link(v.tensor_copy(pos_f, pos_i))
            for m in range(2):
                last = v.tensor_scalar(sin[:, m, :], freq, pos_f[:, m:m + 1], None, ALU.mult)
            link(last)
            turns = rope_a[:, 0:64].rearrange("p (m f) -> p m f", m=2)
            MAGIC = 1.5 * 2 ** 23
            c1 = float(np.float32(201) / 32)
            c2 = float(np.frombuffer((np.array(TWO_PI - c1, np.float32).view(np.uint32) & np.uint32(0xFFFFF000))
                                     .tobytes(), np.float32)[0])
            c3 = float(TWO_PI - c1 - c2)
            for target, quarter in ((cos, 0.25), (sin, 0.0)):
                link(v.tensor_scalar(turns, sin[:], float(1 / TWO_PI), quarter, ALU.mult, ALU.add))
                link(v.tensor_scalar(turns, turns, MAGIC, None, ALU.add))
                link(v.tensor_scalar(turns, turns, MAGIC, None, ALU.subtract))
                src = sin[:]
                for cc in (c1, c2, c3):
                    link(v.scalar_tensor_tensor(target[:], turns, -cc, src, ALU.mult, ALU.add))
                    src = target[:]
                if quarter:
                    link(v.tensor_scalar(target[:], target[:], float(np.pi / 2), None, ALU.add))
                lim = float(np.float32(3.1415925))
                last = v.tensor_scalar(target[:], target[:], lim, -lim, ALU.min, ALU.max)
                if quarter:
                    link(last)
            last.then_inc(ang_ready, 1)

            def ada_tile(n, first, landed):
                kt = n % KT
                dve.wait_ge(ada_landed[n % 2], landed)
                raw = ada_raw[:, n % 2, :]
                if kt == 0:
                    ins = v.tensor_scalar(ada_acc[:], raw, silu_c[:, 0:1], None, ALU.mult)
                else:
                    dve.wait_ge(ada_used, first + 2)
                    ins = v.scalar_tensor_tensor(ada_acc[:], raw, silu_c[:, kt:kt + 1], ada_acc[:], ALU.mult, ALU.add)
                ins.then_inc(ada_used, 1)

            def ada_out(dst, bias, t_value):
                dve.wait_ge(t_full, t_value)
                v.tensor_tensor(dst, T512[:, 0:8], bias, ALU.add).then_inc(t_free, 1)

            with dve.Fori(0, SUPERS) as b:
                for kt in range(KT):
                    if kt == 0:
                        dve.wait_ge(t_full, b + PACKS)
                    ada_tile(kt, b * KT + kt, 16 * (b * (KT // 2) + kt // 2 + 1))
                cols = bass.ds(dve.snap(b * 8), 8)
                ada_out(ada_A[:, cols], bcols[:, 0, cols], b + PACKS + 1)
            close(count)
            dve.wait_ge(x_landed, 16)
            dve.wait_ge(trig_done, 1)

            def lo(at, q, nk, n):
                dve.wait_ge(hi_done, at + q + 1)
                v.tensor_tensor(w_lo[:, q % RING, 0:nk, 0:n], w_raw[:, q % RING, 0:nk, 0:n],
                                w_hi[:, q % RING, 0:nk, 0:n].bitcast(F32), ALU.subtract).then_inc(lo_done, 1)

            def rope(x1, x2, cs_, sn_, ta, tb):
                v.tensor_tensor(ta, x1, sn_, ALU.mult)
                v.tensor_tensor(tb, x2, sn_, ALU.mult)
                v.tensor_tensor(x1, x1, cs_, ALU.mult)
                link(v.tensor_tensor(x2, x2, cs_, ALU.mult))
                v.tensor_tensor(x1, x1, tb, ALU.subtract)
                return v.tensor_tensor(x2, x2, ta, ALU.add)

            def rope_heads(y, col, heads):
                hv = y[:, :, col:col + 128 * heads].rearrange("p m (h d) -> p m h d", h=heads)
                n = 2 * heads * 16
                ta = rope_a[:, 0:n].rearrange("p (m h f) -> p m h f", m=2, h=heads)
                tb = rope_b[:, 0:n].rearrange("p (m h f) -> p m h f", m=2, h=heads)
                cs_, sn_ = bc(cos[:, :, 0:32:2], 2, heads), bc(sin[:, :, 0:32:2], 2, heads)
                return rope(hv[:, :, :, 0:16], hv[:, :, :, 16:32], cs_, sn_, ta, tb)

            def mean_square(l, name, width):
                r = l * RMS_LAYER + (RMS_NO[name] if name != "final" else 0)
                dve.wait_ge(sumsq, 2 * r + 2)
                v.tensor_scalar(ms, ss, 1.0 / width, EPS, ALU.mult, ALU.add).then_inc(meansq, 1)
                dve.wait_ge(rstd_done, r + 1)

            def free_y(l, name):
                k = Y_NO[name]
                if k >= 2:
                    before = Y_NAMES[k - 2]
                    dve.wait_ge(t_full, layer_t(l, T_NO[Y_LAST_T[before]]))
                    if before in Y_LAST_SPLIT:
                        dve.wait_ge(split_done, l * SPLIT_LAYER + SPLIT_NO[Y_LAST_SPLIT[before]] + 1)

            def scaled(l, name, width):
                y = y_slot(Y_NO[name])
                mean_square(l, name, width)
                for m in range(2):
                    last = v.tensor_scalar(y[:, m, 0:width], y[:, m, 0:width], rstd[:, m:m + 1], None, ALU.mult)
                return last

            def evac(l, name):
                i = CI[name]
                a_ = acc[i % 2]
                dve.wait_ge(piece_used, chunk_done(l, name))
                y = y_slot(Y_NO[name]) if name in Y_NO else None
                if y is not None:
                    free_y(l, name)
                done = acc_free[i % 2]
                if name == "nqa":
                    v.tensor_copy(y[:, :, 0:384], a_[:, :, 4:388])
                    v.tensor_tensor(lfa, a_[:, :, 0:4], bc(fbias_l(l), 1, 2), ALU.add).then_inc(done, 1)
                    dve.wait_ge(done, l * PCHUNKS + i // 2 + 2)
                    v.tensor_scalar(lf, lfa, -1.0, None, ALU.mult)
                    last = rope_heads(y, 0, 3)
                    last.then_inc(y_full, 1)
                    v.tensor_tensor(lfb, lf, lfa, ALU.max).then_inc(fz, 1)
                    link(v.tensor_scalar(lfa, lfa, 0.0, None, ALU.min))
                    dve.wait_ge(fe, 2 * l + 2)
                    v.tensor_tensor(lf, lfa, lfb, ALU.subtract).then_inc(fl, 1)
                elif name in ("fq", "fk"):
                    v.tensor_copy(y[:, :, :], a_[:, :, :]).then_inc(y_full, 1)
                    dve.wait_ge(y_full, y_value(l, name))
                    dve.sem_inc(done, 1)
                elif name == "fv":
                    v.tensor_copy(FV, a_[:, :, :]).then_inc(done, 1)
                elif name == "cq":
                    v.tensor_copy(y[:, :, :], a_[:, :, :]).then_inc(done, 1)
                    dve.wait_ge(done, l * PCHUNKS + i // 2 + 2)
                    dve.sem_inc(rms_src, 1)
                    scaled(l, name, 512).then_inc(y_full, 1)
                elif name == "ckv":
                    v.tensor_copy(y[:, :, 0:320], a_[:, :, 0:320]).then_inc(done, 1)
                    dve.wait_ge(done, l * PCHUNKS + i // 2 + 2)
                    dve.sem_inc(rms_src, 1)
                    ta = rope_a[:, 0:64].rearrange("p (m f) -> p m f", m=2)
                    tb = rope_b[:, 0:64].rearrange("p (m f) -> p m f", m=2)
                    link(rope(y[:, :, 256:288], y[:, :, 288:320], cos[:], sin[:], ta, tb))
                    v.tensor_copy(y[:, :, 320:384], y[:, :, 256:320])
                    scaled(l, name, 256).then_inc(y_full, 1)
                elif name == "nqb":
                    v.tensor_copy(y[:, :, :], a_[:, :, :]).then_inc(done, 1)
                    dve.wait_ge(done, l * PCHUNKS + i // 2 + 2)
                    rope_heads(y, 0, 4).then_inc(y_full, 1)
                elif name in ("uq0", "uq1"):
                    for m in range(2):
                        src = a_[:, m, 0:384].rearrange("p (h d) -> p h d", h=2)
                        v.tensor_copy(y[:, m, 0:256].rearrange("p (h d) -> p h d", h=2), src[:, :, 0:128])
                        last = v.tensor_copy(y[:, m, 256:384].rearrange("p (h d) -> p h d", h=2), src[:, :, 128:192])
                    last.then_inc(done, 1)
                    dve.wait_ge(done, l * PCHUNKS + i // 2 + 2)
                    hv = y[:, :, 256:384].rearrange("p m (h d) -> p m h d", h=2)
                    ta = rope_a[:, :].rearrange("p (m h f) -> p m h f", m=2, h=2)
                    tb = rope_b[:, :].rearrange("p (m h f) -> p m h f", m=2, h=2)
                    rope(hv[:, :, :, 0:32], hv[:, :, :, 32:64], bc(cos[:], 2, 2), bc(sin[:], 2, 2), ta, tb
                         ).then_inc(y_full, 1)
                elif name == "kc":
                    v.tensor_copy(y[:, :, 0:384], a_[:, :, 0:384]).then_inc(done, 1)
                    dve.wait_ge(done, l * PCHUNKS + i // 2 + 2)
                    rope_heads(y, 0, 3).then_inc(y_full, 1)
                elif name == "vc":
                    v.tensor_copy(y[:, :, :], a_[:, :, :]).then_inc(done, 1)
                    dve.wait_ge(done, l * PCHUNKS + i // 2 + 2)
                    rope_heads(y, 256, 2).then_inc(y_full, 1)
                elif name in ("kv0", "kv1"):
                    j = int(name[-1])
                    for m in range(2):
                        src = a_[:, m, :].rearrange("p (h d) -> p h d", h=2)
                        v.tensor_copy(y[:, m, 0:256].rearrange("p (h d) -> p h d", h=2), src[:, :, 0:128])
                        last = v.tensor_copy(MV[:, m, 256 * j:256 * j + 256].rearrange("p (h d) -> p h d", h=2),
                                             src[:, :, 128:256])
                    last.then_inc(y_full, 1)
                    dve.wait_ge(y_full, y_value(l, name))
                    dve.sem_inc(done, 1)
                elif name == "vs":
                    v.tensor_copy(VS, a_[:, :, 0:256])
                    v.tensor_copy(y[:, :, 0:256], a_[:, :, 256:512]).then_inc(done, 1)
                    dve.wait_ge(done, l * PCHUNKS + i // 2 + 2)
                    rope_heads(y, 0, 2).then_inc(y_full, 1)
                elif name == "vw":
                    v.tensor_copy(VW, a_[:, :, 0:256])
                    v.tensor_copy(gates.rearrange("p m h r -> p m (h r)"), a_[:, :, 256:280]).then_inc(done, 1)
                    dve.wait_ge(done, l * PCHUNKS + i // 2 + 2)
                    dve.sem_inc(gate_in, 1)
                    dve.wait_ge(gate_e, l + 1)
                    link(v.tensor_scalar_add(gates, gates, 1.0))
                    link(v.reciprocal(gates, gates))
                elif name.startswith("wo"):
                    j = int(name[-1])
                    dve.wait_ge(t_free, layer_t(l, T_NO["gta3"]))
                    residual(a_, GTA, j, done)

            def residual(a_, gate, j, done):
                tmp = ybuf[:, 0]
                link(v.tensor_tensor(tmp[:, :, :], a_[:, :, :], bc(gate[:, 512 * j:512 * j + 512], 1, 2), ALU.mult))
                xs = X[:, :, 512 * j:512 * j + 512]
                v.tensor_tensor(xs, xs, tmp[:, :, :], ALU.add).then_inc(done, 1)

            def y_value(l, name):
                return l * Y_LAYER + Y_NO[name] + 1

            def fbias_l(l):
                return g_fb[:, 0:4]

            g_fb = small[:, 144:148]

            def split(l, name, dst_v, scales, shifts, dst_lo, hi_src):
                dve.wait_ge(t_full, layer_t(l, T_NO[name]))
                for k in range(2):
                    if shifts is None:
                        ins = v.tensor_scalar(dst_v[:, k, :], bank_T[:, k, :], scales[:, k:k + 1], None, ALU.mult)
                    else:
                        ins = v.tensor_scalar(dst_v[:, k, :], bank_T[:, k, :], scales[:, k:k + 1], shifts[:, k:k + 1],
                                              ALU.mult, ALU.add)
                ins.then_inc(t_free, 1)
                dve.wait_ge(v_hi, l * SPLIT_LAYER + SPLIT_NO[name] + 1)
                v.tensor_tensor(dst_lo, dst_v, hi_src.bitcast(F32), ALU.subtract).then_inc(split_done, 1)

            ONSA_T = area(8960, 2048).rearrange("p (h t) -> p h t", h=8)

            def t_out(l, name):
                if name in ("cq0", "cq1"):
                    j = int(name[-1])
                    split(l, name, v_half(Y_NO["cq"], j), g[:, G_Q + 2 * j:G_Q + 2 * j + 2], None,
                          uT_lo[:, 2 * j:2 * j + 2, :], uT_hi[:, 2 * j:2 * j + 2, :])
                elif name == "ckv0":
                    split(l, name, v_half(Y_NO["ckv"], 0), g[:, G_KV:G_KV + 2], None, uT_lo[:, 4:6, :], uT_hi[:, 4:6, :])
                elif name in ("kcT", "vcT"):
                    j = ("kcT", "vcT").index(name)
                    dve.wait_ge(t_full, layer_t(l, T_NO[name]))
                    if j:
                        dve.wait_ge(split_done, l * SPLIT_LAYER + SPLIT_NO["kcT"] + 1)
                    b4 = blk.rearrange("p s (g n) -> p s g n", g=2)
                    v.memset(b4[:, :, :, 15:16], 0.0)
                    for half in range(2):
                        src = bank_T[:, :, 16 * half:16 * half + 240].rearrange("p g (n s) -> p s g n", s=16)
                        pe_ = pos_l[:, j, 16 * half:16 * half + 16]
                        for gi in range(2):
                            ins = v.tensor_tensor(b4[:, 16 * half:16 * half + 16, gi, 0:15], src[:, :, gi, :],
                                                  bc(pe_, 2, 15), ALU.add)
                    ins.then_inc(t_free, 1)
                    dve.wait_ge(v_hi, l * SPLIT_LAYER + SPLIT_NO[name] + 1)
                    B = BLK[j][:, 0:2048].rearrange("p (s r) -> p s r", s=32)
                    v.tensor_tensor(B[:, :, 32:64], blk, B[:, :, 0:32].bitcast(F32), ALU.subtract
                                    ).then_inc(split_done, 1)
                elif name in ("ofox0", "ofox1", "omla0", "omla1") or name.startswith("onsa"):
                    j = int(name[-1])
                    k0 = {"ofox": 4, "omla": 0, "onsa": 8}[name[:4]] + 2 * j
                    src = {"ofox": FQ, "omla": MQ, "onsa": ONSA_T}[name[:4]][:, 2 * j:2 * j + 2, :]
                    split(l, name, src, g[:, G_OUT + k0:G_OUT + k0 + 2], None, hT_lo[:, k0:k0 + 2, :],
                          hT_hi[:, k0:k0 + 2, :])
                elif name.startswith("n1_") or name.startswith("n2_"):
                    k = int(name[3:])
                    if k % 2 == 0 and k + 2 < 8:
                        fill_norm(l, name[:2], k // 2 + 1)
                    sh = ada_A[:, 2 * k:2 * k + 2] if name[1] == "1" else ada_B[:, 16 + 2 * k:18 + 2 * k]
                    split(l, name, v_half(Y_NO[name[:2] + "y0"] + k // 2, k % 2), mscale[:, 2 * k:2 * k + 2], sh,
                          hT_lo[:, 2 * k:2 * k + 2, :], hT_hi[:, 2 * k:2 * k + 2, :])
                elif name.startswith("ada"):
                    b = int(name[3:])
                    ada_out(ada_B[:, 8 * b:8 * b + 8], bcur[:, 8 * b:8 * b + 8], layer_t(l, T_NO[name]))
                elif name == "cum":
                    dve.wait_ge(t_full, layer_t(l, T_NO[name]))
                    v.tensor_copy(cum, bank_T[0:4, 0, :])
                    v.tensor_scalar(ncum, bank_T[0:4, 0, :], -1.0, None, ALU.mult).then_inc(t_free, 1)
                elif name in ("hid0", "hid1"):
                    j = int(name[-1])
                    dve.wait_ge(t_full, layer_t(l, T_NO[name]))
                    v.tensor_copy(hx, T512[:, 0:128]).then_inc(t_free, 1)
                    dve.wait_ge(t_free, layer_t(l, T_NO[name]))
                    link(v.tensor_tensor(ht, hx, hx, ALU.mult))
                    link(v.tensor_scalar(ht, ht, 0.044715, 1.0, ALU.mult, ALU.add))
                    v.tensor_tensor(ht, ht, hx, ALU.mult).then_inc(gelu_in, 1)
                    dve.wait_ge(gelu_t, l * 2 + j + 1)
                    link(v.tensor_scalar(ht, ht, 1.0, 0.5, ALU.add, ALU.mult))
                    v.tensor_tensor(hid.rearrange("p j r -> p (j r)"), ht, hx, ALU.mult).then_inc(hid_done, 1)
                elif name == "kcmp":
                    dve.wait_ge(t_full, layer_t(l, T_NO[name]))
                    v.tensor_copy(kcmp, T512[:, 0:32]).then_inc(t_free, 1)
                elif name == "vcmp":
                    dve.wait_ge(t_full, layer_t(l, T_NO[name]))
                    v.tensor_copy(vcmp, T512[0:32, 0:128]).then_inc(t_free, 1)
                elif name == "vrep":
                    dve.wait_ge(t_full, layer_t(l, T_NO[name]))
                    v.tensor_tensor(VBD, bc(T512[:, 0:128], 1, 8), bc(bmask[:], 2, 128), ALU.mult).then_inc(t_free, 1)
                elif name == "csc":
                    dve.wait_ge(t_full, layer_t(l, T_NO[name]))
                    c4 = cs.rearrange("p (m h n) -> p m h n", m=2, h=8)
                    c3 = cs.rearrange("p (r n) -> p r n", n=16)
                    v.tensor_tensor(c4, T512[:, 0:256].rearrange("p (m h n) -> p m h n", m=2, h=8),
                                    bc(cmask[:], 2, 8), ALU.add).then_inc(t_free, 1)
                    dve.wait_ge(t_free, layer_t(l, T_NO[name]))
                    link(v.tensor_reduce(cmx, c3, AX.X, ALU.max))
                    v.tensor_tensor(c3, c3, bc(cmx, 2, 16), ALU.subtract).then_inc(cmp_x, 1)
                    dve.wait_ge(cmp_e, l + 1)
                    link(v.tensor_reduce(csum, c3, AX.X, ALU.add))
                    link(v.reciprocal(csum, csum))
                    s2 = csum.rearrange("p (m h) -> p m h", m=2)
                    link(v.tensor_tensor(s2, s2, bc(any_ok[:], 2, 8), ALU.mult))
                    link(v.tensor_tensor(s2, s2, gates[:, :, :, 0], ALU.mult))
                    v.tensor_tensor(c3, c3, bc(csum, 2, 16), ALU.mult).then_inc(cmp_p, 1)
                elif name[:2] == "co":
                    j = int(name[2:])
                    m, half = j // 2, j % 2
                    dve.wait_ge(t_full, layer_t(l, T_NO[name]))
                    o = ONSA[:, 4 * half:4 * half + 4, m, :]
                    v.tensor_tensor(o, o, T512.rearrange("p (h n) -> p h n", h=4), ALU.add).then_inc(t_free, 1)
                elif name[:3] in ("gta", "gtm"):
                    n = GATE_ROWS.index(name) + 2
                    if n < 8:
                        dve.wait_ge(t_full, layer_t(l, T_NO[name]))
                        diagonals(l, n)

            def fill_norm(l, which, j):
                name = f"{which}y{j}"
                if j >= 2:
                    free_y(l, name)
                y = y_slot(Y_NO[name])
                for m in range(2):
                    ins = v.tensor_scalar(y[:, m, :], X[:, m, 512 * j:512 * j + 512], rstd[:, m:m + 1], None, ALU.mult)
                ins.then_inc(y_full, 1)

            def norm_o(l, name):
                o, width = {"ofox": (O_FOX, 512), "omla": (O_MLA, 512), "onsa": (ONSA, 1024)}[name]
                if name == "onsa":
                    dve.wait_ge(t_free, layer_t(l, T_NO["co3"]))
                dve.sem_inc(rms_src, 1)
                mean_square(l, name, width)
                for m in range(2):
                    ins = v.tensor_scalar(o[:, :, m, :], o[:, :, m, :], rstd[:, m:m + 1], None, ALU.mult)
                ins.then_inc(o_ready, 1)

            def diagonals(l, n):
                col = (0 if n < 4 else 48) + 4 * (n % 4)
                for k in range(4):
                    ins = v.tensor_scalar(diag[:, 2 + n % 2, 128 * k:128 * k + 128], ident[:],
                                          ada_B[:, col + k:col + k + 1], None, ALU.mult)
                ins.then_inc(diag_done, 1)

            def slot(l, s):
                e = SLOTS[s - 2] if s >= 2 else None
                if e is not None:
                    kind, h = UNITS[e]
                    dve.wait_ge(s_pv, l * NU + e + 1)
                    link(v.reciprocal(fac, psums[:, e % 4, :]))
                    if kind in ("slc", "win"):
                        link(v.tensor_tensor(fac, fac, gates[:, :, h, 1 if kind == "slc" else 2], ALU.mult))
                    o = {"fox": O_FOX, "mla": O_MLA, "slc": ONSA, "win": ONSA}[kind]
                    for m in range(2):
                        if kind == "win":
                            ins = v.scalar_tensor_tensor(o[:, h, m, :], bank_O[:, m, 0:128], fac[:, m:m + 1],
                                                         o[:, h, m, :], ALU.mult, ALU.add)
                        else:
                            ins = v.tensor_scalar(o[:, h, m, :], bank_O[:, m, 0:128], fac[:, m:m + 1], None, ALU.mult)
                    ins.then_inc(s_oev, 1)
                    if e in (3, 7, NU - 1):
                        dve.wait_ge(s_oev, l * NU + e + 1)
                u = SLOTS[s]
                if u is not None:
                    dve.wait_ge(s_scores, l * NU + u + 1)
                    link(v.tensor_tensor(bank_S[:, 0:3:2, :], bank_S[:, 0:3:2, :], bc(causal[:], 1, 2), ALU.add))
                    v.tensor_reduce(nmax[:, u % 4, 0:1], bank_S[:, 0, :], AX.X, ALU.max, negate=True)
                    v.tensor_reduce(nmax[:, u % 4, 1:2], bank_S[:, 1:3, :].rearrange("p a t -> p (a t)"), AX.X,
                                    ALU.max, negate=True).then_inc(s_max, 1)

            def side_piece(l, q):
                i = CHUNK_OF[q]
                lo(l * PIECES, q, CHUNKS[i][5], CHUNKS[i][3])
                for kind, what in STEPS_SIDE.get(q, []):
                    if kind == "T":
                        t_out(l, what)
                    elif kind == "slot":
                        slot(l, what)
                    elif kind == "rms":
                        norm_o(l, what)
                    elif kind == "evac":
                        evac(l, what)
                    elif kind == "diag":
                        diagonals(l, what)
                if q < ADA_FRONT:
                    if q % KT == 0 and q:
                        dve.wait_ge(t_full, layer_t(l, T_NO[f"ada{q // KT - 1}"]))
                    tiles = l * ADA_LAYER + SUPERS * KT + q
                    ada_tile(q, tiles, 16 * (l * (ADA_LAYER // 2) + (SUPERS * KT + q) // 2 + 1))

            dve.sem_inc(rms_src, 1)
            with dve.Fori(0, LAYERS) as l:
                count = region(l * (DVE_FRONT + SUPERS * DVE_SUPER) + DVE_PROLOGUE, DVE_FRONT)
                v.tensor_copy(g[:], gcols[:, bass.ds(l * GAINS, GAINS)])
                v.tensor_copy(g_fb, fbias[:].rearrange("p l h -> p (l h)")[:, bass.ds(l * 4, 4)])
                v.tensor_copy(pos_l[:].rearrange("p k s -> p (k s)"),
                              posT[:].rearrange("p l k s -> p (l k s)")[:, bass.ds(l * 64, 64)])
                link(v.tensor_copy(bcur[:], bcols[:].rearrange("p l n -> p (l n)")[:, bass.ds(l * 96 + 32, 64)]))
                link(v.tensor_scalar_add(mscale[:], ada_A[:, 16:32], 1.0))
                v.tensor_tensor(mscale[:], mscale[:], g[:, G_MIX:G_MIX + 16], ALU.mult)
                mean_square(l, "n1", D)
                fill_norm(l, "n1", 0)
                for n in N1T:
                    t_out(l, n)
                    for q in N1_PIECES[n]:
                        side_piece(l, q)
                for q in range(N1_PIECES[N1T[-1]][-1] + 1, FRONT):
                    side_piece(l, q)
                link(v.tensor_scalar_add(mscale[:], ada_B[:, 32:48], 1.0))
                v.tensor_tensor(mscale[:], mscale[:], g[:, G_MLP:G_MLP + 16], ALU.mult)
                evac(l, "wo3")
                dve.wait_ge(acc_free[1], l * PCHUNKS + len(CHUNKS) // 2 + 1)
                dve.sem_inc(rms_src, 1)
                mean_square(l, "n2", D)
                fill_norm(l, "n2", 0)
                for n in N2T:
                    t_out(l, n)
                close(count)
                with dve.Fori(0, SUPERS) as s:
                    count = region(l * (DVE_FRONT + SUPERS * DVE_SUPER) + DVE_PROLOGUE + DVE_FRONT + s * DVE_SUPER,
                                   DVE_SUPER)
                    at = l * PIECES + FRONT + s * SUPER
                    t0 = l * T_LAYER + T_PROLOGUE + T_FRONT + s * T_SUPER
                    for ch in range(MLP_CHUNKS):
                        for p in range(8):
                            q = ch * 8 + p
                            lo(at, q, 2, 512)
                            if q % 4 == 1:
                                n = q // 4
                                tiles = l * ADA_LAYER + SUPERS * KT + ADA_FRONT + s * KT + n
                                ada_tile(n, tiles, 16 * (l * (ADA_LAYER // 2) + s * (KT // 2)
                                                               + (SUPERS * KT + ADA_FRONT + n) // 2 + 1))
                            j = ch - 1
                            if 0 <= j < 4 and p in (3, 5):
                                t = (p - 3) // 2
                                kt = 4 * j + 2 * t
                                splits = l * SPLIT_LAYER + SPLIT_FRONT + s * 8 + 2 * j + t
                                dve.wait_ge(v_hi, splits + 1)
                                v.tensor_tensor(uT_lo[:, kt:kt + 2, :], v_half(j, t), uT_hi[:, kt:kt + 2, :].bitcast(F32),
                                                ALU.subtract).then_inc(split_done, 1)
                            if 4 <= j and p == 1:
                                dve.wait_ge(piece_used, at + 8 * ch + RING)
                                residual(acc[j % 2], GTM, j - 4, acc_free[j % 2])
                    cols, bias_cols = dve.snap(s * 8), dve.snap(l * -96 + s * 8 + 96)
                    ada_out(ada_A[:, bass.ds(cols, 8)],
                            bcols[:].rearrange("p l n -> p (l n)")[:, bass.ds(bias_cols, 8)], t0 + T_SUPER)
                    dve.wait_ge(piece_used, at + SUPER + RING)
                    residual(acc[1], GTM, 3, acc_free[1])
                    dve.wait_ge(acc_free[1], l * PCHUNKS + len(CHUNKS) // 2 + s * 4 + 5)
                    close(count)
                dve.sem_inc(rms_src, 1)
            mean_square(LAYERS, "final", D)
            dve.wait_ge(fn_landed, 16)
            for m in range(2):
                ins = v.scalar_tensor_tensor(X[:, m, :], X[:, m, :], rstd[:, m:m + 1], FNB, ALU.mult, ALU.mult)
            ins.then_inc(out_ready, 1)

        @block.tensor
        def _(pe):
            pe.sem_inc(piece_used, RING)
            pe.sem_inc(acc_free[0], 1)
            pe.sem_inc(acc_free[1], 1)
            pe.wait_ge(consts, 1)
            pe.wait_ge(packed, 16 * (8 * LAYERS + 1))
            for n, rows in enumerate((LAYERS * GAINS + KT, 96, 96, P)):
                if n:
                    pe.wait_ge(t_free, n)
                pe.transpose(T512[:, 0:rows], diag[0:rows, n, 0:P], ident[0:rows, 0:rows]).then_inc(t_full, 1)

            def t_begin(t):
                pe.wait_ge(t_free, t)

            def ada_sum(t, tiles):
                t_begin(t)
                pe.wait_ge(ada_used, tiles + 2)
                for k in range(8):
                    mm = pe.matmul(T512[:, k:k + 1], ada_acc[:, P * k:P * k + P], ones[:, 0:1], start=True, stop=True)
                mm.then_inc(t_full, 1)

            with pe.Fori(0, SUPERS) as b:
                ada_sum(b + PACKS, b * KT + KT)

            def product(a_, at, q, p, n, per, st_hi, st_lo, k0, first, last):
                pe.wait_ge(lo_done, at + q + 1 + RING)
                for k in range(per):
                    wh, wl = w_hi[:, q % RING, k, 0:n], w_lo[:, q % RING, k, 0:n]
                    kt = k0 + k
                    for m in range(2):
                        tok = slice(P * m, P * m + P)
                        o = a_[:, m, 0:n]
                        pe.matmul(o, st_hi[:, kt, tok], wh, start=first and k == 0, stop=False)
                        pe.matmul(o, st_lo[:, kt, tok], wh, start=False, stop=False)
                        mm = pe.matmul(o, st_hi[:, kt, tok], wl, start=False, stop=last and k == per - 1)
                mm.then_inc(piece_used, 1)

            def turn(l, t, blocks, ready=None):
                t_begin(t)
                if ready is not None:
                    pe.wait_ge(*ready)
                for k, halves in enumerate(blocks):
                    for m in range(2):
                        mm = pe.transpose(bank_T[:, k, P * m:P * m + P], halves[m], ident[:])
                mm.then_inc(t_full, 1)

            def from_y(l, name, cols):
                y = y_slot(Y_NO[name])
                return [[y[:, m, c0:c0 + P] for m in range(2)] for c0 in cols]

            Y_SOURCE = {"nqa0": ("nqa", (0, 128)), "nqa1": ("nqa", (256,)), "fq0": ("fq", (0, 128)),
                        "fq1": ("fq", (256, 384)), "fk0": ("fk", (0, 128)), "fk1": ("fk", (256, 384)),
                        "cq0": ("cq", (0, 128)), "cq1": ("cq", (256, 384)), "ckv0": ("ckv", (0, 128)),
                        "kr": ("ckv", (256,)), "nqb0": ("nqb", (0, 128)), "nqb1": ("nqb", (256, 384)),
                        "uq0n": ("uq0", (0, 128)), "uq0r": ("uq0", (256,)), "nq7": ("kc", (0,)),
                        "kcT": ("kc", (128, 256)), "uq1n": ("uq1", (0, 128)), "uq1r": ("uq1", (256,)),
                        "vcT": ("vc", (0, 128)), "ks": ("vc", (256, 384)), "k0": ("kv0", (0, 128)),
                        "kw": ("vs", (0, 128)), "k1": ("kv1", (0, 128))}

            def t_in(l, name):
                t = layer_t(l, T_NO[name]) - 1
                if name[:3] in ("n1_", "n2_"):
                    k = int(name[3:])
                    yn = f"{name[:2]}y{k // 2}"
                    turn(l, t, from_y(l, yn, [256 * (k % 2), 256 * (k % 2) + 128]),
                         (y_full, l * Y_LAYER + Y_NO[yn] + 1))
                elif name in Y_SOURCE:
                    yn, cols = Y_SOURCE[name]
                    turn(l, t, from_y(l, yn, cols), (y_full, l * Y_LAYER + Y_NO[yn] + 1))
                elif name[:4] in ("ofox", "omla", "onsa"):
                    j = int(name[-1])
                    i = ("ofox", "omla", "onsa").index(name[:4])
                    o = (O_FOX, O_MLA, ONSA)[i]
                    turn(l, t, [[o[:, h, m, :] for m in range(2)] for h in (2 * j, 2 * j + 1)],
                         (o_ready, l * 3 + i + 1))
                elif name.startswith("ada"):
                    ada_sum(t, l * ADA_LAYER + SUPERS * KT + KT * (int(name[3:]) + 1))
                elif name == "cum":
                    t_begin(t)
                    pe.wait_ge(fl, l + 1)
                    pe.matmul(bank_T[0:4, 0, 0:128], lf[:, 0, :], tri[:], start=True, stop=True)
                    pe.matmul(bank_T[0:4, 0, 128:256], lf[:, 0, :], ones[:], start=True, stop=False)
                    pe.matmul(bank_T[0:4, 0, 128:256], lf[:, 1, :], tri[:], start=False, stop=True).then_inc(t_full, 1)
                elif name in ("hid0", "hid1"):
                    t_begin(t)
                    if name == "hid0":
                        pe.wait_ge(hpre_done, l + 1)
                    else:
                        pe.wait_ge(acc_free[CI["cw1"] % 2], l * PCHUNKS + CI["cw1"] // 2 + 2)
                    for j in range(4):
                        mm = pe.matmul(T512[:, 32 * j:32 * j + 32], hpre[:, P * j:P * j + P], I2[:], start=True, stop=True)
                    mm.then_inc(t_full, 1)
                elif name == "kcmp":
                    t_begin(t)
                    pe.wait_ge(hid_done, 2 * l + 1)
                    pe.wait_ge(cw2_landed, 32 * l + 32)
                    for j in range(4):
                        mm = pe.matmul(T512[:, 0:32], cw2[0][:, j, :], hid[:, j, :], start=j == 0, stop=j == 3)
                    mm.then_inc(t_full, 1)
                elif name == "vcmp":
                    t_begin(t)
                    pe.wait_ge(hid_done, 2 * l + 2)
                    for j in range(4):
                        mm = pe.matmul(T512[0:32, 0:128], hid[:, j, :], cw2[1][:, j, :], start=j == 0, stop=j == 3)
                    mm.then_inc(t_full, 1)
                elif name == "vrep":
                    t_begin(t)
                    pe.matmul(T512[:, 0:128], Rsel[:], vcmp, start=True, stop=True).then_inc(t_full, 1)
                elif name == "csc":
                    t_begin(t)
                    for m in range(2):
                        for h in range(8):
                            o = 128 * m + 16 * h
                            mm = pe.matmul(T512[:, o:o + 16], NQ[:, h, P * m:P * m + P],
                                           kcmp[:, 16 * (h // 4):16 * (h // 4) + 16], start=True, stop=True)
                    mm.then_inc(t_full, 1)
                elif name == "cpt":
                    t_begin(t)
                    pe.wait_ge(cmp_p, l + 1)
                    for m in range(2):
                        mm = pe.transpose(T512[:, P * m:P * m + P], cs[:, P * m:P * m + P], ident[:])
                    mm.then_inc(t_full, 1)
                elif name[:2] == "co":
                    m, half = int(name[2:]) // 2, int(name[2:]) % 2
                    t_begin(t)
                    pe.matmul(T512, cpt[:, m, :], VBD[:, 4 * half:4 * half + 4, :].rearrange("p h n -> p (h n)"),
                              start=True, stop=True).then_inc(t_full, 1)
                else:
                    n = GATE_ROWS.index(name)
                    t_begin(t)
                    pe.wait_ge(diag_done, 8 * l + n + 1)
                    pe.matmul(T512, ones[:], diag[:, 2 + n % 2, :], start=True, stop=True).then_inc(t_full, 1)

            def scores(l, u):
                kind, h = UNITS[u]
                if u:
                    pe.wait_ge(s_exp, l * NU + u)
                if u == 0:
                    pe.wait_ge(t_free, layer_t(l, T_NO["fk1"]))
                elif u == 4:
                    pe.wait_ge(t_free, layer_t(l, T_NO["k1"]))
                for m in range(2):
                    qt = slice(P * m, P * m + P)
                    keys = P * (m + 1)
                    o = bank_S[:, 0, :] if m == 0 else bank_S[:, 1:3, :].rearrange("p a t -> p (a t)")
                    if kind == "fox":
                        pe.matmul(o, FQ[:, h, qt], FK[:, h, 0:keys], start=True, stop=False)
                        onehot = ident[0:4, h:h + 1]
                        pe.matmul(o, cum[:, qt], onehot.broadcast_to([4, keys]), start=False, stop=False)
                        mm = pe.matmul(o, onehot.broadcast_to([4, P]), ncum[:, 0:keys], start=False, stop=True)
                    elif kind == "mla":
                        r = 64 * (h % 2)
                        pe.matmul(o, MQ[:, h, qt], MK[:, h, 0:keys], start=True, stop=False)
                        mm = pe.matmul(o, MQR[r:r + 64, h // 2, qt], MKR[r:r + 64, 0:keys], start=False, stop=True)
                    else:
                        k_ = KS if kind == "slc" else KW
                        mm = pe.matmul(o, NQ[:, h, qt], k_[:, h // 4, 0:keys], start=True, stop=True)
                mm.then_inc(s_scores, 1)

            def probs_t(l, u):
                pe.wait_ge(s_exp, l * NU + u + 1)
                if u:
                    pe.wait_ge(s_ptev, l * NU + u)
                for k in range(3):
                    mm = pe.transpose(bank_PT[:, k, :], Pb[:, u % 2, P * k:P * k + P], ident[:])
                mm.then_inc(s_pt, 1)

            def values(l, u):
                kind, h = UNITS[u]
                pe.wait_ge(s_ptev, l * NU + u + 1)
                if u:
                    pe.wait_ge(s_oev, l * NU + u)
                if u == 0:
                    pe.wait_ge(acc_free[CI["fv"] % 2], l * PCHUNKS + CI["fv"] // 2 + 2)
                elif UNITS[u] == ("win", 0):
                    pe.wait_ge(acc_free[CI["vw"] % 2], l * PCHUNKS + CI["vw"] // 2 + 2)
                V, c0 = {"fox": (FV, P * h), "mla": (MV, P * h), "slc": (VS, P * (h // 4)), "win": (VW, P * (h // 4))}[kind]
                v0, v1 = V[:, 0, c0:c0 + P], V[:, 1, c0:c0 + P]
                pt = PTb[:, u % 2, :]
                pe.matmul(bank_O[:, 0, 0:P], pt[:, 0:P], v0, start=True, stop=True)
                pe.matmul(bank_O[:, 1, 0:P], pt[:, P:2 * P], v0, start=True, stop=False)
                pe.matmul(bank_O[:, 1, 0:P], pt[:, 2 * P:3 * P], v1, start=False, stop=True).then_inc(s_pv, 1)

            def slot(l, s):
                if s >= 2 and SLOTS[s - 2] is not None:
                    values(l, SLOTS[s - 2])
                if SLOTS[s] is not None:
                    scores(l, SLOTS[s])
                if s >= 1 and SLOTS[s - 1] is not None:
                    probs_t(l, SLOTS[s - 1])

            with pe.Fori(0, LAYERS) as l:
                t_in(l, "n1_0")
                for i, (name, w, c0, n, kts, per) in enumerate(CHUNKS):
                    a_ = acc[i % 2]
                    splits = l * SPLIT_LAYER + 1
                    pe.wait_ge(acc_free[i % 2], l * PCHUNKS + i // 2 + 1)
                    for p in range(NPIECES[i]):
                        q = FIRST[i] + p
                        if name == "nqa":
                            if p + 1 < 8:
                                t_in(l, f"n1_{p + 1}")
                            pe.wait_ge(split_done, splits + SPLIT_NO[f"n1_{p}"])
                        if name == "uq0" and p == 0:
                            pe.wait_ge(split_done, splits + SPLIT_NO["cq1"])
                        if name == "kv0" and p == 0:
                            pe.wait_ge(split_done, splits + SPLIT_NO["ckv0"])
                        if name == "wo0" and p in (0, 4):
                            pe.wait_ge(split_done, splits + SPLIT_NO["omla1" if p == 0 else "onsa3"])
                        if name == "cw1":
                            j = p // 16
                            if p % 16 == 0:
                                pe.wait_ge(split_done, splits + SPLIT_NO[("kcT", "vcT")[j]])
                            pe.wait_ge(lo_done, l * PIECES + q + 1 + RING)
                            for k in range(2):
                                kt = (p % 16) * 2 + k
                                st = BLK[j][:, 64 * kt:64 * kt + P]
                                pe.matmul(a_[:, j, :], st, w_hi[:, q % RING, k, :], start=kt == 0, stop=False)
                                mm = pe.matmul(a_[:, j, :], st, w_lo[:, q % RING, k, :], start=False, stop=kt == 31)
                            mm.then_inc(piece_used, 1)
                        else:
                            st, k0 = {"w_in": ((hT_hi, hT_lo), 0), "w_out": ((hT_hi, hT_lo), 0), "uq": ((uT_hi, uT_lo), 0),
                                      "ukv": ((uT_hi, uT_lo), 4)}[w]
                            product(a_, l * PIECES, q, p, n, per, st[0], st[1], k0 + p * per, p == 0,
                                    p == NPIECES[i] - 1)
                        for kind, what in STEPS_PE.get(q, []):
                            if kind == "T":
                                t_in(l, what)
                            else:
                                slot(l, what)
                for name in N2T:
                    t_in(l, name)
                with pe.Fori(0, SUPERS) as s:
                    at = l * PIECES + FRONT + s * SUPER
                    t0 = l * T_LAYER + T_PROLOGUE + T_FRONT + s * T_SUPER
                    for ch in range(MLP_CHUNKS):
                        a_ = acc[ch % 2]
                        pe.wait_ge(acc_free[ch % 2], l * PCHUNKS + s * 4 + (len(CHUNKS) + ch) // 2 + 1)
                        for p in range(8):
                            q = ch * 8 + p
                            if q == 0:
                                pe.wait_ge(split_done, l * SPLIT_LAYER + SPLIT_FRONT)
                            st = (hT_hi, hT_lo) if ch < 4 else (uT_hi, uT_lo)
                            if ch == 4:
                                pe.wait_ge(split_done, l * SPLIT_LAYER + SPLIT_FRONT + s * 8 + p + 1)
                            product(a_, at, q, p, 512, 2, st[0], st[1], 2 * p, p == 0, p == 7)
                            j = ch - 1
                            if 0 <= j < 4 and p in (1, 3):
                                t = (p - 1) // 2
                                y = y_slot(j)
                                turn(l, t0 + 2 * j + t,
                                     [[y[:, m, c_:c_ + P] for m in range(2)] for c_ in (256 * t, 256 * t + P)],
                                     (y_full, l * Y_LAYER + Y_FRONT + s * 4 + j + 1))
                            if ch == 7 and p == 5:
                                ada_sum(t0 + 8, l * ADA_LAYER + SUPERS * KT + ADA_FRONT + s * KT + KT)


_INS = ["x", "c", "positions", "inv_freq", "ada_w", "ada_b", "norm_mix", "norm_mlp", "w_in", "fox_b_f", "mla_q_norm",
        "mla_w_uq", "mla_kv_norm", "mla_w_ukv", "nsa_pos_k", "nsa_pos_v", "nsa_cmp_k_w1", "nsa_cmp_k_w2",
        "nsa_cmp_v_w1", "nsa_cmp_v_w2", "out_norm", "w_out", "mlp_w1", "mlp_w2", "final_norm"]


def kernel(**inputs):
    import concourse.bacc as bacc
    from concourse.bass_utils import run_bass_kernel_spmd

    freq = (THETA ** (-np.arange(32) / 32.0)).astype(np.float32).reshape(1, 32)
    nc = bacc.Bacc("TRN2", target_bir_lowering=False, num_devices=1)
    arrays, args = {}, []
    for name in _INS:
        a = freq if name == "inv_freq" else np.ascontiguousarray(inputs[name])
        arrays[f"in_{name}"] = a
        args.append(nc.dram_tensor(f"in_{name}", a.shape, mybir.dt.from_np(a.dtype), kind="ExternalInput").ap())
    args.append(nc.dram_tensor("result", (1, SEQ, D), F32, kind="ExternalOutput").ap())
    trunk(nc, *args)
    r = run_bass_kernel_spmd(nc, [arrays], core_ids=[0])
    return r.results[0]["result"]
```

```python
import numpy as np
from contextlib import ExitStack

import concourse.bass as bass
from concourse import mybir

F32 = mybir.dt.float32
F32R = mybir.dt.float32r
I32 = mybir.dt.int32
ALU = mybir.AluOpType
ACT = mybir.ActivationFunctionType
AX = mybir.AxisListType

P = 128
D = 2048
SEQ = 256
LAYERS = 2
KT = D // P
FF = 4 * D
IN_COLS = 4956
EPS = 1e-6
NEG = -1e30
MLA_SCALE = (128 + 64) ** -0.5
HEAD_SCALE = 128 ** -0.5
THETA = 500000.0
TWO_PI = 2 * np.pi

CHUNKS = [
    ("nqa", "w_in", 2368, 388, 16, 2),
    ("nqb", "w_in", 2756, 512, 16, 2),
    ("kc", "w_in", 3268, 384, 16, 2),
    ("vc", "w_in", 3652, 512, 16, 2),
    ("vs", "w_in", 4164, 512, 16, 2),
    ("vw", "w_in", 4676, 280, 16, 2),
    ("cq", "w_in", 0, 512, 16, 2),
    ("ckv", "w_in", 512, 320, 16, 2),
    ("fq", "w_in", 832, 512, 16, 2),
    ("uq0", "uq", 0, 384, 4, 2),
    ("fk", "w_in", 1344, 512, 16, 2),
    ("uq1", "uq", 384, 384, 4, 2),
    ("fv", "w_in", 1856, 512, 16, 2),
    ("kv0", "ukv", 0, 512, 2, 1),
    ("kv1", "ukv", 512, 512, 2, 1),
    ("cw1", "cw1", 0, 512, 64, 2),
    ("wo0a", "w_out", 0, 512, 8, 2),
    ("wo1a", "w_out", 512, 512, 8, 2),
    ("wo0b", "w_out", 0, 512, 8, 2),
    ("wo1b", "w_out", 512, 512, 8, 2),
    ("wo2", "w_out", 1024, 512, 16, 2),
    ("wo3", "w_out", 1536, 512, 16, 2),
]
OUT_ROWS = [4, 6, 0, 2, 8, 10, 12, 14]


def block_of(name, w, p, per):
    if w == "w_out":
        return OUT_ROWS[p + (4 if name in ("wo0b", "wo1b") else 0)]
    return p * per


CI = {c[0]: i for i, c in enumerate(CHUNKS)}
NPIECES = [c[4] // c[5] for c in CHUNKS]
FIRST = [sum(NPIECES[:i]) for i in range(len(CHUNKS))]
FRONT = sum(NPIECES)
SUPERS = 4
MLP_CHUNKS = 8
SUPER = MLP_CHUNKS * 8
PIECES = FRONT + SUPERS * SUPER
RING = 4
PCHUNKS = (len(CHUNKS) + SUPERS * MLP_CHUNKS) // 2
assert FRONT % RING == 0 and SUPER % RING == 0 and len(CHUNKS) % 2 == 0

ADA_N = 1024
ADA_FRONT = 8 * KT
ADA_LAYER = ADA_FRONT + SUPERS * KT
assert ADA_FRONT <= FRONT
ADA_FIRST = SUPERS * KT
FIRST_RING = 8

UNITS = [("slc", h) for h in range(8)] + [("win", h) for h in range(8)] + \
        [("fox", h) for h in range(4)] + [("mla", h) for h in range(4)]
NU = len(UNITS)
SLOTS = list(range(16)) + [None, None] + list(range(16, NU)) + [None, None]
LAST_NSA, LAST_FOX, LAST_MLA = 15, 19, 23


def piece(name, p):
    return FIRST[CI[name]] + p


STEPS_PE = {}
T_LAG = {}
STEPS_SIDE = {}


def pe_at(q, step):
    STEPS_PE.setdefault(q, []).append(step)


def side_at(q, step):
    STEPS_SIDE.setdefault(q, []).append(step)


def t_step(q, name, lag=2):
    pe_at(q, ("T", name))
    T_LAG[name] = lag


for host, done in (("nqb", "nqa"), ("kc", "nqb"), ("vc", "kc"), ("vs", "vc"), ("vw", "vs"), ("cq", "vw"), ("ckv", "cq"),
                   ("fq", "ckv"), ("uq0", "fq"), ("fk", "uq0"), ("uq1", "fk"), ("fv", "uq1"), ("kv0", "fv"),
                   ("kv1", "kv0"), ("cw1", "kv1"), ("wo1b", "wo0b"), ("wo2", "wo1b"), ("wo3", "wo2")):
    side_at(piece(host, 1), ("evac", done))
for q, name in ((piece("nqb", 2), "nqa0"), (piece("nqb", 4), "nqa1"), (piece("nqb", 6), "cum"),
                (piece("kc", 2), "nqb0"), (piece("kc", 4), "nqb1"), (piece("vc", 2), "nq7"), (piece("vc", 4), "kcT"),
                (piece("vs", 2), "vcT"), (piece("vs", 4), "ks"), (piece("vw", 2), "kw"),
                (piece("ckv", 3), "cq0"), (piece("ckv", 5), "cq1"), (piece("fq", 3), "ckv0"), (piece("fq", 5), "kr"),
                (piece("fk", 0), "fq0"), (piece("fk", 2), "fq1"), (piece("fk", 4), "uq0n"), (piece("fk", 6), "uq0r"),
                (piece("fv", 0), "fk0"), (piece("fv", 2), "fk1"), (piece("fv", 4), "uq1n"), (piece("fv", 6), "uq1r"),
                (piece("cw1", 0), "k0"), (piece("cw1", 2), "k1"),
                (piece("cw1", 20), "ofox0"), (piece("cw1", 22), "ofox1"), (piece("cw1", 24), "hid0"),
                (piece("cw1", 26), "kcmp"), (piece("cw1", 28), "csc"), (piece("cw1", 30), "cpt")):
    t_step(q, name)
side_at(piece("cw1", 18), ("rms", "ofox"))
side_at(piece("cw1", 17), ("hpre", 0))
for s, q in enumerate([piece("vw", 2) + (14 * k) // 5 for k in range(18)]
                      + [piece("cw1", 0) + 3 * k for k in range(10)]):
    pe_at(q, ("slot", s))
    side_at(q + 3, ("slot", s))
assert len(SLOTS) == 28
W = piece("wo0a", 0)
side_at(W, ("rms", "omla"))
t_step(W, "omla0", lag=1)
t_step(W, "omla1", lag=1)
side_at(W + 1, ("hpre", 1))
for q, name in ((W + 2, "hid1"), (W + 3, "vcmp"), (W + 4, "vrep"), (W + 4, "co0"), (W + 4, "co1"), (W + 5, "co2"),
                (W + 5, "co3")):
    t_step(q, name, lag=1)
side_at(W + 6, ("rms", "onsa"))
for name in ("onsa0", "onsa1", "onsa2", "onsa3"):
    t_step(W + 7, name, lag=1)
side_at(W + 8, ("diag", 0))
side_at(W + 8, ("diag", 1))
for j in range(4):
    t_step(W + 9 + j, f"gta{j}")
    t_step(W + 14 + 2 * j, f"gtm{j}")

ADA_AT = []
for q in range(FRONT):
    c = CHUNKS[sum(q >= f for f in FIRST) - 1]
    if len(ADA_AT) < ADA_FRONT and not (c[1] == "cw1" and (q - FIRST[CI["cw1"]]) % 3 == 2) and c[1] != "ukv":
        if ADA_AT and len(ADA_AT) % KT == 0 and q < ADA_AT[-1] + 2:
            continue
        ADA_AT.append(q)
assert len(ADA_AT) == ADA_FRONT and ADA_AT[-1] + 2 < FRONT
ADA_NO = {q: n for n, q in enumerate(ADA_AT)}
ADA_BLOCKS = [0, 1, 6, 7, 2, 3, 4, 5]
for b in range(8):
    t_step(ADA_AT[KT * b + KT - 1], f"ada{b}")
GATE_ROWS = [f"gta{j}" for j in range(4)] + [f"gtm{j}" for j in range(4)]

CHUNK_OF = [i for i in range(len(CHUNKS)) for p in range(NPIECES[i])]
N1_PIECES = {f"n1_{k}": [k + 2] for k in range(2, 8)}
N1_PIECES["n1_0"], N1_PIECES["n1_1"] = [], list(range(4))

KINDS = ["evac", "hpre", "T", "slot", "rms", "diag"]
last = 0
for q in range(FRONT):
    for kind, name in STEPS_PE.get(q, []):
        if kind == "T":
            last = max(last, q + T_LAG[name])
            side_at(last, ("T", name))
for steps in STEPS_SIDE.values():
    steps.sort(key=lambda step: KINDS.index(step[0]))

N1T = [f"n1_{k}" for k in range(8)]
N2T = [f"n2_{k}" for k in range(8)]
T_NAMES = N1T + [s[1] for q in range(FRONT) for s in STEPS_PE.get(q, []) if s[0] == "T"] + N2T
T_NO = {n: i for i, n in enumerate(T_NAMES)}
T_FRONT = len(T_NAMES)
T_SUPER = 9
T_LAYER = T_FRONT + SUPERS * T_SUPER
T_PROLOGUE = 4 + 4
PACKS = 4

Y_NAMES = [f"n1y{j}" for j in range(4)] + ["nqa", "nqb", "kc", "vc", "vs", "cq", "ckv", "fq", "uq0",
                                           "fk", "uq1", "kv0", "kv1"] + [f"n2y{j}" for j in range(4)]
Y_NO = {n: i for i, n in enumerate(Y_NAMES)}
Y_FRONT = len(Y_NAMES)
Y_LAYER = Y_FRONT + SUPERS * 4
Y_LAST_T = {"nqa": "nqa1", "fq": "fq1", "fk": "fk1", "cq": "cq1", "ckv": "kr", "nqb": "nqb1", "uq0": "uq0r",
            "kc": "kcT", "uq1": "uq1r", "vc": "ks", "kv0": "k0", "vs": "kw", "kv1": "k1"}
for j in range(4):
    Y_LAST_T[f"n1y{j}"] = f"n1_{2 * j + 1}"
    Y_LAST_T[f"n2y{j}"] = f"n2_{2 * j + 1}"
Y_LAST_SPLIT = {"cq": "cq1", "ckv": "ckv0"}
for j in range(4):
    Y_LAST_SPLIT[f"n1y{j}"] = f"n1_{2 * j + 1}"
    Y_LAST_SPLIT[f"n2y{j}"] = f"n2_{2 * j + 1}"
SPLIT_NAMES = [n for n in T_NAMES if n[:2] in ("n1", "n2") or n in
               ("cq0", "cq1", "ckv0", "kcT", "vcT", "ofox0", "ofox1", "omla0", "omla1",
                "onsa0", "onsa1", "onsa2", "onsa3")]
SPLIT_NO = {n: i for i, n in enumerate(SPLIT_NAMES)}
SPLIT_FRONT = len(SPLIT_NAMES)
SPLIT_LAYER = SPLIT_FRONT + SUPERS * 8
RMS_NAMES = ["n1", "cq", "ckv", "ofox", "omla", "onsa", "n2"]
RMS_NO = {n: i for i, n in enumerate(RMS_NAMES)}
RMS_LAYER = len(RMS_NAMES)

GAINS = 54
G_MIX, G_MLP, G_OUT, G_Q, G_KV = 0, 16, 32, 48, 52

DVE_PROLOGUE, DVE_FRONT, DVE_SUPER = 30, 260, 20


def trunk(nc, x, c, positions, inv_freq, ada_w, ada_b, norm_mix, norm_mlp, w_in, fox_b_f, mla_q_norm, mla_w_uq,
          mla_kv_norm, mla_w_ukv, nsa_pos_k, nsa_pos_v, cmp_k_w1, cmp_k_w2, cmp_v_w1, cmp_v_w2,
          out_norm, w_out, mlp_w1, mlp_w2, final_norm, out):
    with ExitStack() as ctx:
        def sb(name, shape, dt=F32):
            return ctx.enter_context(nc.sbuf_tensor(name, shape, dt))

        def sem(name):
            return ctx.enter_context(nc.semaphore(name))

        X = sb("X", [P, 2, D])
        hT_hi, hT_lo = sb("hT_hi", [P, KT, SEQ], F32R), sb("hT_lo", [P, KT, SEQ], F32R)
        uT_hi, uT_lo = sb("uT_hi", [P, KT, SEQ], F32R), sb("uT_lo", [P, KT, SEQ], F32R)
        w_raw = sb("w_raw", [P, RING, 2, 512])
        w_hi, w_lo = sb("w_hi", [P, RING, 2, 512], F32R), sb("w_lo", [P, RING, 2, 512], F32R)
        ada_raw = sb("ada_raw", [P, 2, ADA_N])
        ada_acc = sb("ada_acc", [P, ADA_N])
        ybuf = sb("ybuf", [P, 2, 2, 512])
        arena = sb("arena", [P, 12544])
        ident, ones, tri, causal = sb("ident", [P, P]), sb("ones", [P, P]), sb("tri", [P, P]), sb("causal", [P, P])
        gcols = sb("gcols", [P, LAYERS * GAINS + KT])
        bcols = sb("bcols", [P, LAYERS, 96])
        posT = sb("posT", [P, LAYERS, 2, 32])
        g = sb("g", [P, GAINS])
        ada_A = sb("ada_A", [P, 32])
        ada_B = sb("ada_B", [P, 64])
        mscale = sb("mscale", [P, KT])
        silu_c = sb("silu_c", [P, KT])
        bcur = sb("bcur", [P, 64])
        pos_l = sb("pos_l", [P, 2, 32])
        cos, sin = sb("cos", [P, 2, 32]), sb("sin", [P, 2, 32])
        rope_a, rope_b = sb("rope_a", [P, P]), sb("rope_b", [P, P])
        cum = sb("cum", [4, SEQ])
        nident = sb("nident", [4, 4])
        fbias = sb("fbias", [P, LAYERS, 4])
        cmask = sb("cmask", [P, 2, 16])
        any_ok = sb("any_ok", [P, 2])
        Rsel = sb("Rsel", [32, P])
        I2 = sb("I2", [64, 32])
        bmask = sb("bmask", [P, 8])
        small = sb("small", [P, 160])
        ss, ms, rstd, mhalf = small[:, 0:2], small[:, 2:4], small[:, 4:6], small[:, 6:8]
        pos_f = small[:, 8:10]
        nmax = small[:, 16:24].rearrange("p (u b) -> p u b", u=4)
        psums = small[:, 24:32].rearrange("p (u b) -> p u b", u=4)
        fac = small[:, 32:34]
        lf = small[:, 40:48].rearrange("p (m h) -> p m h", m=2)
        lfa = small[:, 48:56].rearrange("p (m h) -> p m h", m=2)
        lfb = small[:, 56:64].rearrange("p (m h) -> p m h", m=2)
        gates = small[:, 64:112].rearrange("p (m h r) -> p m h r", m=2, h=8)
        cmx, csum = small[:, 112:128], small[:, 128:144]

        def area(at, n):
            return arena[:, at:at + n]

        FQ = area(0, 1024).rearrange("p (h t) -> p h t", h=4)
        FK = area(1024, 1024).rearrange("p (h t) -> p h t", h=4)
        FV = area(2048, 1024).rearrange("p (m n) -> p m n", m=2)
        KS = area(4864, 512).rearrange("p (g t) -> p g t", g=2)
        KW = area(5376, 512).rearrange("p (g t) -> p g t", g=2)
        VS = area(5888, 512).rearrange("p (m n) -> p m n", m=2)
        VW = area(6400, 512).rearrange("p (m n) -> p m n", m=2)
        MQ = area(3072, 1024).rearrange("p (h t) -> p h t", h=4)
        MQR = area(4096, 512).rearrange("p (a t) -> p a t", a=2)
        MKR = area(4608, 256)
        MK = area(4864, 1024).rearrange("p (h t) -> p h t", h=4)
        MV = area(5888, 1024).rearrange("p (m n) -> p m n", m=2)
        NQ = area(6912, 2048).rearrange("p (h t) -> p h t", h=8)
        ONSA = area(8960, 2048).rearrange("p (h m n) -> p h m n", h=8, m=2)
        Pb = area(11008, 768).rearrange("p (u n) -> p u n", u=2)
        PTb = area(11776, 768).rearrange("p (u n) -> p u n", u=2)
        junk = area(0, 1024)
        blk = area(8960, 1024).rearrange("p (l r) -> p l r", l=32)
        hpre = arena[0:64, 1024:1536]
        hid = area(0, 128).rearrange("p (j r) -> p j r", j=4)
        hx, ht = area(128, 128), area(256, 128)
        cs = area(384, 256)
        cpt = area(640, 256).rearrange("p (m q) -> p m q", m=2)
        kcmp = area(896, 32)
        vcmp = arena[0:32, 4096:4224]
        cw2 = [area(2048, 512).rearrange("p (j n) -> p j n", j=4), area(2560, 512).rearrange("p (j n) -> p j n", j=4)]
        VBD = area(4864, 1024).rearrange("p (h n) -> p h n", h=8)
        GTA = area(6912, 2048)
        GTM = area(1024, 2048)
        FNB = area(6912, 2048)
        O_FOX = area(0, 1024).rearrange("p (h m n) -> p h m n", h=4, m=2)
        O_MLA = area(3072, 1024).rearrange("p (h m n) -> p h m n", h=4, m=2)
        uflat_hi = uT_hi[:, :, :].rearrange("p k t -> p (k t)")
        uflat_lo = uT_lo[:, :, :].rearrange("p k t -> p (k t)")
        BLK = [uflat_hi[:, 1536:1536 + 33 * 64], uflat_lo[:, 1536:1536 + 33 * 64]]
        diag = ybuf[:, :, :, :].rearrange("p b m n -> p (b m) n")
        junk_y = ybuf[:, :, :, :].rearrange("p b m n -> p (b m n)")

        first_raw = area(0, FIRST_RING * ADA_N).rearrange("p (r n) -> p r n", r=FIRST_RING)

        acc = [ctx.enter_context(nc.psum_tensor(f"acc{i}", [P, 2, 512], F32)) for i in range(2)]
        bank_S = ctx.enter_context(nc.psum_tensor("bank_S", [P, 4, P], F32))
        bank_PT = ctx.enter_context(nc.psum_tensor("bank_PT", [P, 4, P], F32))
        bank_O = ctx.enter_context(nc.psum_tensor("bank_O", [P, 2, SEQ], F32))
        bank_T = ctx.enter_context(nc.psum_tensor("bank_T", [P, 2, SEQ], F32))
        T512 = bank_T[:, :, :].rearrange("p a t -> p (a t)")

        loaded = sem("loaded")
        packed = sem("packed")
        consts = sem("consts")
        raw_landed = [sem(f"raw_landed{i}") for i in range(RING)]
        hi_done, lo_done, piece_used = sem("hi_done"), sem("lo_done"), sem("piece_used")
        acc_free = [sem("acc_free0"), sem("acc_free1")]
        ada_landed = [sem("ada_landed0"), sem("ada_landed1")]
        first_landed = [sem(f"first_landed{i}") for i in range(FIRST_RING)]
        ada_used = sem("ada_used")
        t_full, t_free = sem("t_full"), sem("t_free")
        y_full = sem("y_full")
        v_hi, split_done = sem("v_hi"), sem("split_done")
        x_landed, out_ready = sem("x_landed"), sem("out_ready")
        sumsq, meansq, rstd_done = sem("sumsq"), sem("meansq"), sem("rstd_done")
        rms_src = sem("rms_src")
        s_scores, s_max, s_exp = sem("s_scores"), sem("s_max"), sem("s_exp")
        s_pt, s_ptev, s_pv, s_oev = sem("s_pt"), sem("s_ptev"), sem("s_pv"), sem("s_oev")
        fz, fe, fl = sem("fz"), sem("fe"), sem("fl")
        gate_in, gate_e = sem("gate_in"), sem("gate_e")
        gelu_in, gelu_t, hid_done = sem("gelu_in"), sem("gelu_t"), sem("hid_done")
        hpre_done = sem("hpre_done")
        cmp_x, cmp_e, cmp_p = sem("cmp_x"), sem("cmp_e"), sem("cmp_p")
        cw2_landed = sem("cw2_landed")
        fn_landed = sem("fn_landed")
        diag_done = sem("diag_done")
        o_ready = sem("o_ready")
        dve_own, pool_own = sem("dve_own"), sem("pool_own")
        stored = sem("stored")
        silu_e, ang_ready, trig_done = sem("silu_e"), sem("ang_ready"), sem("trig_done")

        w_dram = {"w_in": (w_in.rearrange("l k n -> (l k) n"), D), "uq": (mla_w_uq.rearrange("l k n -> (l k) n"), 512),
                  "ukv": (mla_w_ukv.rearrange("l k n -> (l k) n"), 256),
                  "w_out": (w_out.rearrange("l k n -> (l k) n"), D)}
        cw1_dram = [cmp_k_w1.rearrange("l k n -> (l k) n"), cmp_v_w1.rearrange("l k n -> (l k) n")]
        cw2_dram = [cmp_k_w2.rearrange("l k n -> (l k) n"), cmp_v_w2.rearrange("l k n -> (l k) n")]
        w1_dram = mlp_w1.rearrange("l k n -> (l k) n")
        w2_dram = mlp_w2.rearrange("l k n -> (l k) n")
        ada_dram = ada_w.rearrange("l k n -> (l k) n")
        x_dram = x.rearrange("a (m p) d -> p (a m) d", p=P)
        out_dram = out.rearrange("a (m p) d -> p (a m) d", p=P)

        def layer_t(l, n):
            return l * T_LAYER + T_PROLOGUE + n + 1

        def used(l, q):
            return l * PIECES + q + 1 + RING

        def chunk_done(l, name):
            return used(l, FIRST[CI[name]] + NPIECES[CI[name]] - 1)

        def y_slot(n):
            return ybuf[:, n % 2]

        def v_half(n, t):
            return ybuf[:, n % 2, :, 256 * t:256 * t + 256]

        block = ctx.enter_context(nc.Block())

        @block.sync
        def _(sp):
            def ada_tile(at, first_row, col, n):
                row, col = sp.snap(first_row), sp.snap(col)
                sp.wait_ge(ada_used, at + n + FIRST_RING - 1)
                sp.dma_start(ada_raw[:, n % 2, :], ada_dram[bass.ds(row, P), bass.ds(col, ADA_N)]
                             ).then_inc(ada_landed[n % 2], 16)

            with sp.Fori(0, SUPERS) as b:
                for kt in range(KT):
                    col = sp.snap(b * ADA_N)
                    sp.wait_ge(ada_used, b * KT + kt + 1)
                    sp.dma_start(first_raw[:, kt % FIRST_RING, :], ada_dram[kt * P:kt * P + P, bass.ds(col, ADA_N)]
                                 ).then_inc(first_landed[kt % FIRST_RING], 16)

            def put(at, q, weights, row, nk, col, n):
                if type(col) is int:
                    width = weights.shape[1]
                    start = sp.snap(row * width)
                    src = weights.rearrange("k n -> (k n)")[bass.ds(start, nk * P * width)]
                    src = src.rearrange("(k n) -> k n", n=width)[:, col:col + n]
                else:
                    row, col = sp.snap(row), sp.snap(col)
                    src = weights[bass.ds(row, nk * P), bass.ds(col, n)]
                sp.wait_ge(lo_done, at + q + 1)
                sp.dma_start(w_raw[:, q % RING, 0:nk, 0:n], src.rearrange("(k p) n -> p k n", p=P)
                             ).then_inc(raw_landed[q % RING], 16)

            with sp.Fori(0, LAYERS) as l:
                for i, (name, w, c0, n, kts, per) in enumerate(CHUNKS):
                    for p in range(NPIECES[i]):
                        q = FIRST[i] + p
                        if w == "cw1":
                            put(l * PIECES, q, cw1_dram[p // 16], l * 4096 + (p % 16) * 256, 2, 0, 512)
                        else:
                            weights, k = w_dram[w]
                            block_row = block_of(name, w, p, per) * P
                            row = (l + 1) * k + (block_row - k) if name == "cq" else l * k + block_row
                            put(l * PIECES, q, weights, row, per, c0, n)
                        if q - 1 in ADA_NO:
                            n_ada = ADA_NO[q - 1]
                            ada_tile(l * ADA_LAYER + SUPERS * KT, l * D + (n_ada % KT) * P,
                                     4096 + ADA_BLOCKS[n_ada // KT] * ADA_N, n_ada)
                        if q == piece("cw1", 24):
                            sp.wait_ge(s_oev, l * NU + LAST_FOX + 1)
                            for j in range(2):
                                sp.dma_start(cw2[j], cw2_dram[j][bass.ds(l * 512, 512), :]
                                             .rearrange("(k p) n -> p k n", p=P)).then_inc(cw2_landed, 16)
                with sp.Fori(0, SUPERS) as s:
                    for ch in range(MLP_CHUNKS):
                        for p in range(8):
                            q = ch * 8 + p
                            at = l * PIECES + FRONT + s * SUPER
                            if ch < 4:
                                put(at, q, w1_dram, l * D + p * 256, 2, s * D + ch * 512, 512)
                            else:
                                put(at, q, w2_dram, l * FF + s * D + p * 256, 2, (ch - 4) * 512, 512)
                            if q % 4 == 1:
                                ada_tile(l * ADA_LAYER + SUPERS * KT + ADA_FRONT + s * KT,
                                         l * -D + D + (q // 4) * P, s * ADA_N, q // 4)
            sp.wait_ge(sumsq, 2 * LAYERS * RMS_LAYER)
            sp.dma_start(FNB, final_norm.rearrange("(a n) -> a n", a=1).broadcast_to([P, D])).then_inc(fn_landed, 16)
            sp.wait_ge(out_ready, 1)
            sp.dma_start(out_dram, X[:, :, :]).then_inc(stored, 16)
            sp.wait_ge(stored, 16)

        @block.gpsimd
        def _(pool):
            n = 0
            gp = nc.gpsimd

            def link(ins):
                nonlocal n
                n += 1
                ins.then_inc(pool_own, 1)
                pool.wait_ge(pool_own, n)

            def select(out_, fill, base, pattern, mult, op=ALU.is_ge):
                link(gp.affine_select(out=out_, in_=out_, compare_op=op, fill=fill, base=base, pattern=pattern,
                                      channel_multiplier=mult))

            link(gp.memset(ident[:], 0.0))
            select(ident[:], 1.0, 0, [[-1, P]], 1, ALU.not_equal)
            link(gp.memset(nident[:], 0.0))
            select(nident[:], -1.0, 0, [[-1, 4]], 1, ALU.not_equal)
            link(gp.memset(ones[:], 1.0))
            link(gp.memset(mhalf, -0.5))
            link(gp.memset(tri[:], 1.0))
            select(tri[:], 0.0, 0, [[1, P]], -1)
            link(gp.memset(causal[:], 0.0))
            select(causal[:], NEG, 0, [[-1, P]], 1)
            link(gp.memset(cmask[:], 0.0))
            select(cmask[:], NEG, -31, [[P, 2], [-16, 16]], 1)
            link(gp.memset(cmask[:, :, 15:16], NEG))
            link(gp.memset(any_ok[:], 1.0))
            select(any_ok[:], 0.0, -31, [[P, 2]], 1)
            link(gp.memset(bmask[:], 1.0))
            select(bmask[:], 0.0, 0, [[-16, 8]], 1)
            select(bmask[:], 0.0, 15, [[16, 8]], -1)
            link(gp.memset(Rsel[:], 0.0))
            r4 = Rsel[:].rearrange("r (g h n) -> r g h n", g=2, h=4)
            select(r4, 1.0, 0, [[-16, 2], [0, 4], [-1, 16]], 1, ALU.not_equal)
            link(gp.memset(I2[:], 0.0))
            select(I2[:], 1.0, 0, [[-1, 32]], 1, ALU.not_equal)
            select(I2[:], 1.0, -32, [[-1, 32]], 1, ALU.not_equal)
            link(gp.memset(uT_hi[:, 6:16, :].bitcast(F32), 0.0))
            gp.memset(uT_lo[:, 6:16, :].bitcast(F32), 0.0).then_inc(consts, 1)
            with pool.Fori(0, RMS_LAYER * LAYERS + 1) as r:
                pool.wait_ge(meansq, r + 1)
                gp.tensor_tensor(rstd, ms, mhalf, ALU.pow).then_inc(rstd_done, 1)

        @block.scalar
        def _(act):
            a = nc.scalar

            rows = diag[:, :, 0:P]
            for l in range(LAYERS):
                o = l * GAINS
                for v, at, n in ((norm_mix, G_MIX, 16), (norm_mlp, G_MLP, 16), (out_norm, G_OUT, 16),
                                 (mla_q_norm, G_Q, 4), (mla_kv_norm, G_KV, 2)):
                    act.dma_start(rows[o + at:o + at + n, 0, :], v[l].rearrange("(k p) -> k p", p=P)).then_inc(packed, 16)
                act.dma_start(rows[0:96, 1 + l, :], ada_b[l].rearrange("(k p) -> k p", p=P)).then_inc(packed, 16)
                act.dma_start(rows[64 * l:64 * l + 32, 3, :], nsa_pos_k[l]).then_inc(packed, 16)
                act.dma_start(rows[64 * l + 32:64 * l + 64, 3, :], nsa_pos_v[l]).then_inc(packed, 16)
            o = LAYERS * GAINS
            act.dma_start(rows[o:o + KT, 0, :], c[0].rearrange("(k p) -> k p", p=P)).then_inc(packed, 16)

            act.dma_start(rope_b[:, 0:2].bitcast(I32), positions.rearrange("a (m p) -> p (a m)", p=P),
                         allow_slow_non_contiguous=True
                         ).then_inc(loaded, 16)
            act.dma_start(rope_b[:, 32:64], inv_freq.broadcast_to([P, 32])).then_inc(loaded, 16)
            act.dma_start(fbias[:, :, :].rearrange("p l h -> p (l h)"),
                         fox_b_f.rearrange("(a l) h -> a (l h)", a=1).broadcast_to([P, LAYERS * 4])).then_inc(loaded, 16)
            act.dma_start(X[:, :, :], x_dram).then_inc(x_landed, 16)

            act.wait_ge(t_free, 1)
            a.activation(silu_c[:], gcols[:, LAYERS * GAINS:], ACT.Exp, scale=-1.0).then_inc(silu_e, 1)
            act.wait_ge(ang_ready, 1)
            a.activation(cos[:], cos[:], ACT.Sin)
            a.activation(sin[:], sin[:], ACT.Sin).then_inc(trig_done, 1)

            def hi(at, q, nk, n):
                act.wait_ge(raw_landed[q % RING], landed_value(at, q))
                act.wait_ge(piece_used, at[0] * PIECES + at[1] * SUPER + at[2] + q + 1)
                a.activation(w_hi[:, q % RING, 0:nk, 0:n], w_raw[:, q % RING, 0:nk, 0:n], ACT.Copy).then_inc(hi_done, 1)

            def landed_value(at, q):
                return 16 * (at[0] * (PIECES // RING) + at[1] * (SUPER // RING) + at[2] // RING + q // RING + 1)

            def square_sum(l, name, srcs, junks):
                r = l * RMS_LAYER + (RMS_NO[name] if name != "final" else 0)
                for m in range(2):
                    if m:
                        act.wait_ge(sumsq, 2 * r + 1)
                    a.activation(junks[m], srcs[m], ACT.Square, accum_out=ss[:, m:m + 1]).then_inc(sumsq, 1)

            def split_hi(l, name, v, dst):
                act.wait_ge(t_free, layer_t(l, T_NO[name]))
                a.activation(dst, v, ACT.Copy).then_inc(v_hi, 1)

            def turn_out(l, name, dst, n, scale=1.0):
                act.wait_ge(t_full, layer_t(l, T_NO[name]))
                a.activation(dst, T512[:, 0:n], ACT.Copy, scale=scale).then_inc(t_free, 1)

            def flat(ap):
                return ap.rearrange("p a t -> p (a t)")

            def t_out(l, name):
                if name in ("nqa0", "nqa1", "nqb0", "nqb1", "nq7"):
                    h0, n = {"nqa0": (0, 2), "nqa1": (2, 1), "nqb0": (3, 2), "nqb1": (5, 2), "nq7": (7, 1)}[name]
                    turn_out(l, name, flat(NQ[:, h0:h0 + n, :]), n * SEQ, HEAD_SCALE)
                elif name in ("fq0", "fq1"):
                    j = int(name[-1])
                    turn_out(l, name, flat(FQ[:, 2 * j:2 * j + 2, :]), 512, HEAD_SCALE)
                elif name in ("fk0", "fk1"):
                    j = int(name[-1])
                    turn_out(l, name, flat(FK[:, 2 * j:2 * j + 2, :]), 512)
                elif name in ("uq0n", "uq1n"):
                    j = int(name[2])
                    turn_out(l, name, flat(MQ[:, 2 * j:2 * j + 2, :]), 512, MLA_SCALE)
                elif name in ("uq0r", "uq1r"):
                    turn_out(l, name, MQR[:, int(name[2]), :], SEQ, MLA_SCALE)
                elif name in ("k0", "k1"):
                    j = int(name[-1])
                    turn_out(l, name, flat(MK[:, 2 * j:2 * j + 2, :]), 512)
                elif name == "kr":
                    turn_out(l, name, MKR, SEQ)
                elif name == "ks":
                    turn_out(l, name, flat(KS), 512)
                elif name == "kw":
                    turn_out(l, name, flat(KW), 512)
                elif name in ("cq0", "cq1"):
                    j = int(name[-1])
                    split_hi(l, name, v_half(Y_NO["cq"], j), uT_hi[:, 2 * j:2 * j + 2, :])
                elif name == "ckv0":
                    split_hi(l, name, v_half(Y_NO["ckv"], 0), uT_hi[:, 4:6, :])
                elif name in ("kcT", "vcT"):
                    j = ("kcT", "vcT").index(name)
                    split_hi(l, name, blk, BLK[j][:, 0:2048].rearrange("p (l r) -> p l r", l=32)[:, :, 0:32])
                elif name in ("ofox0", "ofox1"):
                    j = int(name[-1])
                    split_hi(l, name, FQ[:, 2 * j:2 * j + 2, :], hT_hi[:, 4 + 2 * j:6 + 2 * j, :])
                elif name in ("omla0", "omla1"):
                    j = int(name[-1])
                    split_hi(l, name, MQ[:, 2 * j:2 * j + 2, :], hT_hi[:, 2 * j:2 * j + 2, :])
                elif name.startswith("onsa"):
                    j = int(name[-1])
                    split_hi(l, name, ONSA_T[:, 2 * j:2 * j + 2, :], hT_hi[:, 8 + 2 * j:10 + 2 * j, :])
                elif name.startswith("n1_") or name.startswith("n2_"):
                    k = int(name[3:])
                    split_hi(l, name, v_half(Y_NO[name[0:2] + "y0"] + k // 2, k % 2), hT_hi[:, 2 * k:2 * k + 2, :])
                elif name in ("hid0", "hid1"):
                    j = int(name[-1])
                    act.wait_ge(gelu_in, l * 2 + j + 1)
                    a.activation(ht, ht, ACT.Tanh, scale=float(np.sqrt(2 / np.pi))).then_inc(gelu_t, 1)
                elif name == "csc":
                    act.wait_ge(cmp_x, l + 1)
                    a.activation(cs, cs, ACT.Exp).then_inc(cmp_e, 1)
                elif name == "cpt":
                    turn_out(l, name, flat(cpt), 256)
                elif name[:3] in ("gta", "gtm"):
                    j = int(name[-1])
                    dst = GTA if name[:3] == "gta" else GTM
                    act.wait_ge(t_full, layer_t(l, T_NO[name]))
                    a.activation(dst[:, 512 * j:512 * j + 512], T512, ACT.Copy).then_inc(t_free, 1)

            def slot(l, s):
                u = SLOTS[s]
                b = SLOTS[s - 1] if s >= 1 else None
                if b is not None:
                    act.wait_ge(s_pt, l * NU + b + 1)
                    a.activation(PTb[:, b % 2, :], bank_PT[:, 0:3, :].rearrange("p a t -> p (a t)"), ACT.Copy
                                 ).then_inc(s_ptev, 1)
                if u is not None:
                    act.wait_ge(s_max, l * NU + u + 1)
                    a.activation(Pb[:, u % 2, 0:128], bank_S[:, 0, :], ACT.Exp, bias=nmax[:, u % 4, 0:1],
                                 accum_out=psums[:, u % 4, 0:1])
                    a.activation(Pb[:, u % 2, 128:384], bank_S[:, 1:3, :].rearrange("p a t -> p (a t)"), ACT.Exp,
                                 bias=nmax[:, u % 4, 1:2], accum_out=psums[:, u % 4, 1:2]).then_inc(s_exp, 1)

            ONSA_T = area(8960, 2048).rearrange("p (h t) -> p h t", h=8)

            def rms(l, name):
                act.wait_ge(rms_src, l * RMS_LAYER + RMS_NO[name] + 1)
                if name in ("n1", "n2"):
                    srcs, junks = [X[:, m, :] for m in range(2)], [junk_y] * 2
                elif name == "cq":
                    srcs, junks = [y_slot(Y_NO["cq"])[:, m, 0:512] for m in range(2)], [junk[:, 0:512]] * 2
                elif name == "ckv":
                    srcs, junks = [y_slot(Y_NO["ckv"])[:, m, 0:256] for m in range(2)], [junk[:, 0:256]] * 2
                elif name == "onsa":
                    srcs = [ONSA[:, :, m, :] for m in range(2)]
                    junks = [junk_y[:, 0:1024].rearrange("p (h n) -> p h n", h=8)] * 2
                else:
                    o = O_FOX if name == "ofox" else O_MLA
                    srcs = [o[:, :, m, :] for m in range(2)]
                    junks = [junk_y[:, 0:512].rearrange("p (h n) -> p h n", h=4)] * 2
                square_sum(l, name, srcs, junks)

            def side_piece(l, q):
                i = CHUNK_OF[q]
                hi((l, 0, 0), q, CHUNKS[i][5], CHUNKS[i][3])
                for kind, what in STEPS_SIDE.get(q, []):
                    if kind == "T":
                        t_out(l, what)
                    elif kind == "slot":
                        slot(l, what)
                    elif kind == "rms":
                        rms(l, what)
                    elif kind == "evac" and what in ("cq", "ckv"):
                        rms(l, what)
                    elif kind == "evac" and what == "nqa":
                        act.wait_ge(fz, l + 1)
                        a.activation(lfb, lfb, ACT.Exp, scale=-1.0).then_inc(fe, 1)
                        act.wait_ge(fe, 2 * l + 1)
                        a.activation(lfb, lfb, ACT.Ln, bias=1.0).then_inc(fe, 1)
                    elif kind == "evac" and what == "vw":
                        act.wait_ge(gate_in, l + 1)
                        a.activation(gates[:, :, :, :], gates[:, :, :, :], ACT.Exp, scale=-1.0).then_inc(gate_e, 1)
                    elif kind == "hpre":
                        act.wait_ge(piece_used, used(l, piece("cw1", 15 + 16 * what)))
                        if what:
                            act.wait_ge(t_full, layer_t(l, T_NO["hid0"]))
                        a.activation(hpre, acc[CI["cw1"] % 2][0:64, what, :], ACT.Copy
                                     ).then_inc(acc_free[CI["cw1"] % 2] if what else hpre_done, 1)

            def mlp_part(l, s, end):
                at = (l, s, FRONT)
                for q in range(2, end):
                    ch, p = q // 8, q % 8
                    hi(at, q, 2, 512)
                    j = ch - 1
                    if 0 <= j < 4:
                        ydone = l * Y_LAYER + Y_FRONT + s * 4 + j
                        splits = l * SPLIT_LAYER + SPLIT_FRONT + s * 8
                        tdone = l * T_LAYER + T_PROLOGUE + T_FRONT + s * T_SUPER + 2 * j
                        if p == 1:
                            act.wait_ge(piece_used, l * PIECES + s * SUPER + FRONT + 8 * ch + RING)
                            if j == 0:
                                act.wait_ge(acc_free[1], l * PCHUNKS + s * 4 + len(CHUNKS) // 2 + 1)
                            if j >= 2:
                                act.wait_ge(split_done, splits + 2 * (j - 1))
                            a.activation(y_slot(j)[:, :, :], acc[j % 2][:, :, :], ACT.Relu).then_inc(y_full, 1)
                            act.wait_ge(y_full, ydone + 1)
                            act.sem_inc(acc_free[j % 2], 1)
                        if p in (3, 5):
                            t = (p - 3) // 2
                            act.wait_ge(t_full, tdone + t + 1)
                            a.activation(v_half(j, t), bank_T[:, :, :], ACT.Square).then_inc(t_free, 1)
                            act.wait_ge(t_free, tdone + t + 1)
                            kt = 4 * j + 2 * t
                            a.activation(uT_hi[:, kt:kt + 2, :], v_half(j, t), ACT.Copy).then_inc(v_hi, 1)

            with act.Fori(0, LAYERS) as l:
                rms(l, "n1")
                for n in N1T:
                    t_out(l, n)
                    for q in N1_PIECES[n]:
                        side_piece(l, q)
                for q in range(N1_PIECES[N1T[-1]][-1] + 1, FRONT):
                    side_piece(l, q)
                rms(l, "n2")
                for n in N2T:
                    t_out(l, n)
                    if n in ("n2_6", "n2_7"):
                        hi((l, 0, FRONT), N2T.index(n) - 6, 2, 512)
                with act.Fori(0, SUPERS - 1) as s:
                    mlp_part(l, s, SUPER + 2)
                mlp_part(l, SUPERS - 1, SUPER)
            act.wait_ge(rms_src, LAYERS * RMS_LAYER + 1)
            square_sum(LAYERS, "final", [X[:, m, :] for m in range(2)], [junk_y] * 2)

        @block.vector
        def _(dve):
            v = nc.vector
            own = [0, 0]

            def link(ins):
                own[0] += 1
                ins.then_inc(dve_own, 1)
                dve.wait_ge(dve_own, own[1] + own[0])

            def region(base, count):
                own[0], own[1] = 0, base
                return count

            def close(count):
                assert own[0] <= count, own
                if count > own[0]:
                    dve.sem_inc(dve_own, count - own[0])

            def bc(ap, axis, n):
                ap = ap.unsqueeze(axis)
                shape = list(ap.shape)
                shape[axis] = n
                return ap.broadcast_to(shape)

            count = region(0, DVE_PROLOGUE)
            dve.sem_inc(lo_done, RING)
            dve.sem_inc(ada_used, FIRST_RING)
            dve.wait_ge(t_full, 1)
            v.tensor_copy(gcols[:], T512[:, 0:LAYERS * GAINS + KT]).then_inc(t_free, 1)
            for l in range(LAYERS):
                dve.wait_ge(t_full, 2 + l)
                v.tensor_copy(bcols[:, l, :], T512[:, 0:96]).then_inc(t_free, 1)
            dve.wait_ge(t_full, 4)
            v.tensor_copy(posT[:].rearrange("p l k s -> p (l k s)"), T512[:, 0:P]).then_inc(t_free, 1)
            dve.wait_ge(silu_e, 1)
            link(v.tensor_scalar_add(silu_c[:], silu_c[:], 1.0))
            link(v.reciprocal(silu_c[:], silu_c[:]))
            dve.wait_ge(t_free, 1)
            link(v.tensor_tensor(silu_c[:], silu_c[:], gcols[:, LAYERS * GAINS:], ALU.mult))
            dve.wait_ge(loaded, 48)
            pos_i = rope_b[:, 0:2].bitcast(I32)
            freq = rope_b[:, 32:64]
            link(v.tensor_copy(pos_f, pos_i))
            for m in range(2):
                last = v.tensor_scalar(sin[:, m, :], freq, pos_f[:, m:m + 1], None, ALU.mult)
            link(last)
            turns = rope_a[:, 0:64].rearrange("p (m f) -> p m f", m=2)
            MAGIC = 1.5 * 2 ** 23
            c1 = float(np.float32(201) / 32)
            c2 = float(np.frombuffer((np.array(TWO_PI - c1, np.float32).view(np.uint32) & np.uint32(0xFFFFF000))
                                     .tobytes(), np.float32)[0])
            c3 = float(TWO_PI - c1 - c2)
            for target, quarter in ((cos, 0.25), (sin, 0.0)):
                link(v.tensor_scalar(turns, sin[:], float(1 / TWO_PI), quarter, ALU.mult, ALU.add))
                link(v.tensor_scalar(turns, turns, MAGIC, None, ALU.add))
                link(v.tensor_scalar(turns, turns, MAGIC, None, ALU.subtract))
                src = sin[:]
                for cc in (c1, c2, c3):
                    link(v.scalar_tensor_tensor(target[:], turns, -cc, src, ALU.mult, ALU.add))
                    src = target[:]
                if quarter:
                    link(v.tensor_scalar(target[:], target[:], float(np.pi / 2), None, ALU.add))
                lim = float(np.float32(3.1415925))
                last = v.tensor_scalar(target[:], target[:], lim, -lim, ALU.min, ALU.max)
                if quarter:
                    link(last)
            last.then_inc(ang_ready, 1)

            def ada_tile(kt, raw, tiles):
                if kt == 0:
                    ins = v.tensor_scalar(ada_acc[:], raw, silu_c[:, 0:1], None, ALU.mult)
                else:
                    dve.wait_ge(ada_used, tiles + FIRST_RING)
                    ins = v.scalar_tensor_tensor(ada_acc[:], raw, silu_c[:, kt:kt + 1], ada_acc[:], ALU.mult, ALU.add)
                ins.then_inc(ada_used, 1)

            def ada_out(dst, bias, t_value):
                dve.wait_ge(t_full, t_value)
                v.tensor_tensor(dst, T512[:, 0:8], bias, ALU.add).then_inc(t_free, 1)

            dve.wait_ge(x_landed, 16)
            dve.sem_inc(rms_src, 1)
            with dve.Fori(0, SUPERS) as b:
                for kt in range(KT):
                    if kt == 0:
                        dve.wait_ge(t_full, b + PACKS)
                    dve.wait_ge(first_landed[kt % FIRST_RING], 16 * (b * (KT // FIRST_RING) + kt // FIRST_RING + 1))
                    ada_tile(kt, first_raw[:, kt % FIRST_RING, :], b * KT + kt)
                cols = bass.ds(dve.snap(b * 8), 8)
                ada_out(ada_A[:, cols], bcols[:, 0, cols], b + PACKS + 1)
            close(count)
            dve.wait_ge(trig_done, 1)

            def lo(at, q, nk, n):
                dve.wait_ge(hi_done, at + q + 1)
                v.tensor_tensor(w_lo[:, q % RING, 0:nk, 0:n], w_raw[:, q % RING, 0:nk, 0:n],
                                w_hi[:, q % RING, 0:nk, 0:n].bitcast(F32), ALU.subtract).then_inc(lo_done, 1)

            def rope(x1, x2, cs_, sn_, ta, tb):
                v.tensor_tensor(ta, x1, sn_, ALU.mult)
                v.tensor_tensor(tb, x2, sn_, ALU.mult)
                v.tensor_tensor(x1, x1, cs_, ALU.mult)
                link(v.tensor_tensor(x2, x2, cs_, ALU.mult))
                v.tensor_tensor(x1, x1, tb, ALU.subtract)
                return v.tensor_tensor(x2, x2, ta, ALU.add)

            def rope_heads(y, col, heads):
                hv = y[:, :, col:col + 128 * heads].rearrange("p m (h d) -> p m h d", h=heads)
                n = 2 * heads * 16
                ta = rope_a[:, 0:n].rearrange("p (m h f) -> p m h f", m=2, h=heads)
                tb = rope_b[:, 0:n].rearrange("p (m h f) -> p m h f", m=2, h=heads)
                cs_, sn_ = bc(cos[:, :, 0:32:2], 2, heads), bc(sin[:, :, 0:32:2], 2, heads)
                return rope(hv[:, :, :, 0:16], hv[:, :, :, 16:32], cs_, sn_, ta, tb)

            def mean_square(l, name, width):
                r = l * RMS_LAYER + (RMS_NO[name] if name != "final" else 0)
                dve.wait_ge(sumsq, 2 * r + 2)
                v.tensor_scalar(ms, ss, 1.0 / width, EPS, ALU.mult, ALU.add).then_inc(meansq, 1)
                dve.wait_ge(rstd_done, r + 1)

            def free_y(l, name):
                k = Y_NO[name]
                if k >= 2:
                    before = Y_NAMES[k - 2]
                    dve.wait_ge(t_full, layer_t(l, T_NO[Y_LAST_T[before]]))
                    if before in Y_LAST_SPLIT:
                        dve.wait_ge(split_done, l * SPLIT_LAYER + SPLIT_NO[Y_LAST_SPLIT[before]] + 1)

            def scaled(l, name, width):
                y = y_slot(Y_NO[name])
                mean_square(l, name, width)
                for m in range(2):
                    last = v.tensor_scalar(y[:, m, 0:width], y[:, m, 0:width], rstd[:, m:m + 1], None, ALU.mult)
                return last

            def evac(l, name):
                i = CI[name]
                a_ = acc[i % 2]
                dve.wait_ge(piece_used, chunk_done(l, name))
                y = y_slot(Y_NO[name]) if name in Y_NO else None
                if y is not None:
                    free_y(l, name)
                done = acc_free[i % 2]
                if name == "nqa":
                    v.tensor_copy(y[:, :, 0:384], a_[:, :, 4:388])
                    v.tensor_tensor(lfa, a_[:, :, 0:4], bc(fbias_l(l), 1, 2), ALU.add).then_inc(done, 1)
                    dve.wait_ge(done, l * PCHUNKS + i // 2 + 2)
                    v.tensor_scalar(lf, lfa, -1.0, None, ALU.mult)
                    last = rope_heads(y, 0, 3)
                    last.then_inc(y_full, 1)
                    v.tensor_tensor(lfb, lf, lfa, ALU.max).then_inc(fz, 1)
                    link(v.tensor_scalar(lfa, lfa, 0.0, None, ALU.min))
                    dve.wait_ge(fe, 2 * l + 2)
                    v.tensor_tensor(lf, lfa, lfb, ALU.subtract).then_inc(fl, 1)
                elif name in ("fq", "fk"):
                    v.tensor_copy(y[:, :, :], a_[:, :, :]).then_inc(y_full, 1)
                    dve.wait_ge(y_full, y_value(l, name))
                    dve.sem_inc(done, 1)
                elif name == "fv":
                    v.tensor_copy(FV, a_[:, :, :]).then_inc(done, 1)
                elif name == "cq":
                    v.tensor_copy(y[:, :, :], a_[:, :, :]).then_inc(done, 1)
                    dve.wait_ge(done, l * PCHUNKS + i // 2 + 2)
                    dve.sem_inc(rms_src, 1)
                    scaled(l, name, 512).then_inc(y_full, 1)
                elif name == "ckv":
                    v.tensor_copy(y[:, :, 0:320], a_[:, :, 0:320]).then_inc(done, 1)
                    dve.wait_ge(done, l * PCHUNKS + i // 2 + 2)
                    dve.sem_inc(rms_src, 1)
                    ta = rope_a[:, 0:64].rearrange("p (m f) -> p m f", m=2)
                    tb = rope_b[:, 0:64].rearrange("p (m f) -> p m f", m=2)
                    link(rope(y[:, :, 256:288], y[:, :, 288:320], cos[:], sin[:], ta, tb))
                    v.tensor_copy(y[:, :, 320:384], y[:, :, 256:320])
                    scaled(l, name, 256).then_inc(y_full, 1)
                elif name == "nqb":
                    v.tensor_copy(y[:, :, :], a_[:, :, :]).then_inc(done, 1)
                    dve.wait_ge(done, l * PCHUNKS + i // 2 + 2)
                    rope_heads(y, 0, 4).then_inc(y_full, 1)
                elif name in ("uq0", "uq1"):
                    for m in range(2):
                        src = a_[:, m, 0:384].rearrange("p (h d) -> p h d", h=2)
                        v.tensor_copy(y[:, m, 0:256].rearrange("p (h d) -> p h d", h=2), src[:, :, 0:128])
                        last = v.tensor_copy(y[:, m, 256:384].rearrange("p (h d) -> p h d", h=2), src[:, :, 128:192])
                    last.then_inc(done, 1)
                    dve.wait_ge(done, l * PCHUNKS + i // 2 + 2)
                    hv = y[:, :, 256:384].rearrange("p m (h d) -> p m h d", h=2)
                    ta = rope_a[:, :].rearrange("p (m h f) -> p m h f", m=2, h=2)
                    tb = rope_b[:, :].rearrange("p (m h f) -> p m h f", m=2, h=2)
                    rope(hv[:, :, :, 0:32], hv[:, :, :, 32:64], bc(cos[:], 2, 2), bc(sin[:], 2, 2), ta, tb
                         ).then_inc(y_full, 1)
                elif name == "kc":
                    v.tensor_copy(y[:, :, 0:384], a_[:, :, 0:384]).then_inc(done, 1)
                    dve.wait_ge(done, l * PCHUNKS + i // 2 + 2)
                    rope_heads(y, 0, 3).then_inc(y_full, 1)
                elif name == "vc":
                    v.tensor_copy(y[:, :, :], a_[:, :, :]).then_inc(done, 1)
                    dve.wait_ge(done, l * PCHUNKS + i // 2 + 2)
                    rope_heads(y, 256, 2).then_inc(y_full, 1)
                elif name in ("kv0", "kv1"):
                    j = int(name[-1])
                    if j == 0:
                        dve.wait_ge(s_pv, l * NU + LAST_NSA + 1)
                    for m in range(2):
                        src = a_[:, m, :].rearrange("p (h d) -> p h d", h=2)
                        v.tensor_copy(y[:, m, 0:256].rearrange("p (h d) -> p h d", h=2), src[:, :, 0:128])
                        last = v.tensor_copy(MV[:, m, 256 * j:256 * j + 256].rearrange("p (h d) -> p h d", h=2),
                                             src[:, :, 128:256])
                    last.then_inc(y_full, 1)
                    dve.wait_ge(y_full, y_value(l, name))
                    dve.sem_inc(done, 1)
                elif name == "vs":
                    v.tensor_copy(VS, a_[:, :, 0:256])
                    v.tensor_copy(y[:, :, 0:256], a_[:, :, 256:512]).then_inc(done, 1)
                    dve.wait_ge(done, l * PCHUNKS + i // 2 + 2)
                    rope_heads(y, 0, 2).then_inc(y_full, 1)
                elif name == "vw":
                    v.tensor_copy(VW, a_[:, :, 0:256])
                    v.tensor_copy(gates.rearrange("p m h r -> p m (h r)"), a_[:, :, 256:280]).then_inc(done, 1)
                    dve.wait_ge(done, l * PCHUNKS + i // 2 + 2)
                    dve.sem_inc(gate_in, 1)
                    dve.wait_ge(gate_e, l + 1)
                    link(v.tensor_scalar_add(gates, gates, 1.0))
                    link(v.reciprocal(gates, gates))
                elif name.startswith("wo"):
                    j = int(name[2])
                    dve.wait_ge(t_free, layer_t(l, T_NO["gta3"]))
                    residual(a_, GTA, j, done)

            def residual(a_, gate, j, done):
                tmp = ybuf[:, 0]
                link(v.tensor_tensor(tmp[:, :, :], a_[:, :, :], bc(gate[:, 512 * j:512 * j + 512], 1, 2), ALU.mult))
                xs = X[:, :, 512 * j:512 * j + 512]
                v.tensor_tensor(xs, xs, tmp[:, :, :], ALU.add).then_inc(done, 1)

            def y_value(l, name):
                return l * Y_LAYER + Y_NO[name] + 1

            def fbias_l(l):
                return g_fb[:, 0:4]

            g_fb = small[:, 144:148]

            def split(l, name, dst_v, scales, shifts, dst_lo, hi_src):
                dve.wait_ge(t_full, layer_t(l, T_NO[name]))
                for k in range(2):
                    if shifts is None:
                        ins = v.tensor_scalar(dst_v[:, k, :], bank_T[:, k, :], scales[:, k:k + 1], None, ALU.mult)
                    else:
                        ins = v.tensor_scalar(dst_v[:, k, :], bank_T[:, k, :], scales[:, k:k + 1], shifts[:, k:k + 1],
                                              ALU.mult, ALU.add)
                ins.then_inc(t_free, 1)
                dve.wait_ge(v_hi, l * SPLIT_LAYER + SPLIT_NO[name] + 1)
                v.tensor_tensor(dst_lo, dst_v, hi_src.bitcast(F32), ALU.subtract).then_inc(split_done, 1)

            ONSA_T = area(8960, 2048).rearrange("p (h t) -> p h t", h=8)

            def t_out(l, name):
                if name in ("cq0", "cq1"):
                    j = int(name[-1])
                    split(l, name, v_half(Y_NO["cq"], j), g[:, G_Q + 2 * j:G_Q + 2 * j + 2], None,
                          uT_lo[:, 2 * j:2 * j + 2, :], uT_hi[:, 2 * j:2 * j + 2, :])
                elif name == "ckv0":
                    split(l, name, v_half(Y_NO["ckv"], 0), g[:, G_KV:G_KV + 2], None, uT_lo[:, 4:6, :], uT_hi[:, 4:6, :])
                elif name in ("kcT", "vcT"):
                    j = ("kcT", "vcT").index(name)
                    dve.wait_ge(t_full, layer_t(l, T_NO[name]))
                    if j:
                        dve.wait_ge(split_done, l * SPLIT_LAYER + SPLIT_NO["kcT"] + 1)
                    b4 = blk.rearrange("p s (g n) -> p s g n", g=2)
                    v.memset(b4[:, :, :, 15:16], 0.0)
                    for half in range(2):
                        src = bank_T[:, :, 16 * half:16 * half + 240].rearrange("p g (n s) -> p s g n", s=16)
                        pe_ = pos_l[:, j, 16 * half:16 * half + 16]
                        for gi in range(2):
                            ins = v.tensor_tensor(b4[:, 16 * half:16 * half + 16, gi, 0:15], src[:, :, gi, :],
                                                  bc(pe_, 2, 15), ALU.add)
                    ins.then_inc(t_free, 1)
                    dve.wait_ge(v_hi, l * SPLIT_LAYER + SPLIT_NO[name] + 1)
                    B = BLK[j][:, 0:2048].rearrange("p (s r) -> p s r", s=32)
                    v.tensor_tensor(B[:, :, 32:64], blk, B[:, :, 0:32].bitcast(F32), ALU.subtract
                                    ).then_inc(split_done, 1)
                elif name in ("ofox0", "ofox1", "omla0", "omla1") or name.startswith("onsa"):
                    j = int(name[-1])
                    k0 = {"ofox": 4, "omla": 0, "onsa": 8}[name[:4]] + 2 * j
                    src = {"ofox": FQ, "omla": MQ, "onsa": ONSA_T}[name[:4]][:, 2 * j:2 * j + 2, :]
                    split(l, name, src, g[:, G_OUT + k0:G_OUT + k0 + 2], None, hT_lo[:, k0:k0 + 2, :],
                          hT_hi[:, k0:k0 + 2, :])
                elif name.startswith("n1_") or name.startswith("n2_"):
                    k = int(name[3:])
                    if k % 2 == 0 and k + 2 < 8:
                        fill_norm(l, name[:2], k // 2 + 1)
                    sh = ada_A[:, 2 * k:2 * k + 2] if name[1] == "1" else ada_B[:, 16 + 2 * k:18 + 2 * k]
                    split(l, name, v_half(Y_NO[name[:2] + "y0"] + k // 2, k % 2), mscale[:, 2 * k:2 * k + 2], sh,
                          hT_lo[:, 2 * k:2 * k + 2, :], hT_hi[:, 2 * k:2 * k + 2, :])
                elif name.startswith("ada"):
                    b = ADA_BLOCKS[int(name[3:])]
                    ada_out(ada_B[:, 8 * b:8 * b + 8], bcur[:, 8 * b:8 * b + 8], layer_t(l, T_NO[name]))
                elif name == "cum":
                    dve.wait_ge(t_full, layer_t(l, T_NO[name]))
                    v.tensor_copy(cum[:], bank_T[0:4, 0, :]).then_inc(t_free, 1)
                elif name in ("hid0", "hid1"):
                    j = int(name[-1])
                    dve.wait_ge(t_full, layer_t(l, T_NO[name]))
                    v.tensor_copy(hx, T512[:, 0:128]).then_inc(t_free, 1)
                    dve.wait_ge(t_free, layer_t(l, T_NO[name]))
                    link(v.tensor_tensor(ht, hx, hx, ALU.mult))
                    link(v.tensor_scalar(ht, ht, 0.044715, 1.0, ALU.mult, ALU.add))
                    v.tensor_tensor(ht, ht, hx, ALU.mult).then_inc(gelu_in, 1)
                    dve.wait_ge(gelu_t, l * 2 + j + 1)
                    link(v.tensor_scalar(ht, ht, 1.0, 0.5, ALU.add, ALU.mult))
                    v.tensor_tensor(hid.rearrange("p j r -> p (j r)"), ht, hx, ALU.mult).then_inc(hid_done, 1)
                elif name == "kcmp":
                    dve.wait_ge(t_full, layer_t(l, T_NO[name]))
                    v.tensor_copy(kcmp, T512[:, 0:32]).then_inc(t_free, 1)
                elif name == "vcmp":
                    dve.wait_ge(t_full, layer_t(l, T_NO[name]))
                    v.tensor_copy(vcmp, T512[0:32, 0:128]).then_inc(t_free, 1)
                elif name == "vrep":
                    dve.wait_ge(t_full, layer_t(l, T_NO[name]))
                    v.tensor_tensor(VBD, bc(T512[:, 0:128], 1, 8), bc(bmask[:], 2, 128), ALU.mult).then_inc(t_free, 1)
                elif name == "csc":
                    dve.wait_ge(t_full, layer_t(l, T_NO[name]))
                    c4 = cs.rearrange("p (m h n) -> p m h n", m=2, h=8)
                    c3 = cs.rearrange("p (r n) -> p r n", n=16)
                    v.tensor_tensor(c4, T512[:, 0:256].rearrange("p (m h n) -> p m h n", m=2, h=8),
                                    bc(cmask[:], 2, 8), ALU.add).then_inc(t_free, 1)
                    dve.wait_ge(t_free, layer_t(l, T_NO[name]))
                    link(v.tensor_reduce(cmx, c3, AX.X, ALU.max))
                    v.tensor_tensor(c3, c3, bc(cmx, 2, 16), ALU.subtract).then_inc(cmp_x, 1)
                    dve.wait_ge(cmp_e, l + 1)
                    link(v.tensor_reduce(csum, c3, AX.X, ALU.add))
                    link(v.reciprocal(csum, csum))
                    s2 = csum.rearrange("p (m h) -> p m h", m=2)
                    link(v.tensor_tensor(s2, s2, bc(any_ok[:], 2, 8), ALU.mult))
                    link(v.tensor_tensor(s2, s2, gates[:, :, :, 0], ALU.mult))
                    v.tensor_tensor(c3, c3, bc(csum, 2, 16), ALU.mult).then_inc(cmp_p, 1)
                elif name[:2] == "co":
                    j = int(name[2:])
                    m, half = j // 2, j % 2
                    dve.wait_ge(t_full, layer_t(l, T_NO[name]))
                    o = ONSA[:, 4 * half:4 * half + 4, m, :]
                    v.tensor_tensor(o, o, T512.rearrange("p (h n) -> p h n", h=4), ALU.add).then_inc(t_free, 1)
                elif name[:3] in ("gta", "gtm"):
                    n = GATE_ROWS.index(name) + 2
                    if n < 8:
                        dve.wait_ge(t_full, layer_t(l, T_NO[name]))
                        diagonals(l, n)

            def fill_norm(l, which, j):
                name = f"{which}y{j}"
                if j >= 2:
                    free_y(l, name)
                y = y_slot(Y_NO[name])
                for m in range(2):
                    ins = v.tensor_scalar(y[:, m, :], X[:, m, 512 * j:512 * j + 512], rstd[:, m:m + 1], None, ALU.mult)
                ins.then_inc(y_full, 1)

            def norm_o(l, name):
                o, width = {"ofox": (O_FOX, 512), "omla": (O_MLA, 512), "onsa": (ONSA, 1024)}[name]
                if name == "onsa":
                    dve.wait_ge(t_free, layer_t(l, T_NO["co3"]))
                dve.sem_inc(rms_src, 1)
                mean_square(l, name, width)
                for m in range(2):
                    ins = v.tensor_scalar(o[:, :, m, :], o[:, :, m, :], rstd[:, m:m + 1], None, ALU.mult)
                ins.then_inc(o_ready, 1)

            def diagonals(l, n):
                col = (0 if n < 4 else 48) + 4 * (n % 4)
                for k in range(4):
                    ins = v.tensor_scalar(diag[:, 2 + n % 2, 128 * k:128 * k + 128], ident[:],
                                          ada_B[:, col + k:col + k + 1], None, ALU.mult)
                ins.then_inc(diag_done, 1)

            def slot(l, s):
                e = SLOTS[s - 2] if s >= 2 else None
                if e is not None:
                    kind, h = UNITS[e]
                    dve.wait_ge(s_pv, l * NU + e + 1)
                    link(v.reciprocal(fac, psums[:, e % 4, :]))
                    if kind in ("slc", "win"):
                        link(v.tensor_tensor(fac, fac, gates[:, :, h, 1 if kind == "slc" else 2], ALU.mult))
                    o = {"fox": O_FOX, "mla": O_MLA, "slc": ONSA, "win": ONSA}[kind]
                    for m in range(2):
                        if kind == "win":
                            ins = v.scalar_tensor_tensor(o[:, h, m, :], bank_O[:, m, 0:128], fac[:, m:m + 1],
                                                         o[:, h, m, :], ALU.mult, ALU.add)
                        else:
                            ins = v.tensor_scalar(o[:, h, m, :], bank_O[:, m, 0:128], fac[:, m:m + 1], None, ALU.mult)
                    ins.then_inc(s_oev, 1)
                    if e in (LAST_NSA, LAST_FOX, LAST_MLA):
                        dve.wait_ge(s_oev, l * NU + e + 1)
                u = SLOTS[s]
                if u is not None:
                    dve.wait_ge(s_scores, l * NU + u + 1)
                    link(v.tensor_tensor(bank_S[:, 0:3:2, :], bank_S[:, 0:3:2, :], bc(causal[:], 1, 2), ALU.add))
                    v.tensor_reduce(nmax[:, u % 4, 0:1], bank_S[:, 0, :], AX.X, ALU.max, negate=True)
                    v.tensor_reduce(nmax[:, u % 4, 1:2], bank_S[:, 1:3, :].rearrange("p a t -> p (a t)"), AX.X,
                                    ALU.max, negate=True).then_inc(s_max, 1)

            def side_piece(l, q):
                i = CHUNK_OF[q]
                lo(l * PIECES, q, CHUNKS[i][5], CHUNKS[i][3])
                for kind, what in STEPS_SIDE.get(q, []):
                    if kind == "T":
                        t_out(l, what)
                    elif kind == "slot":
                        slot(l, what)
                    elif kind == "rms":
                        norm_o(l, what)
                    elif kind == "evac":
                        evac(l, what)
                    elif kind == "diag":
                        diagonals(l, what)
                if q in ADA_NO:
                    n = ADA_NO[q]
                    dve.wait_ge(ada_landed[n % 2], 16 * (l * (ADA_LAYER // 2) + n // 2 + 1))
                    ada_tile(n % KT, ada_raw[:, n % 2, :], l * ADA_LAYER + ADA_FIRST + n)

            def mlp_piece(l, s, q):
                lo(l * PIECES + FRONT + s * SUPER, q, 2, 512)
                if q % 4 == 1:
                    n = q // 4
                    dve.wait_ge(ada_landed[n % 2], 16 * (l * (ADA_LAYER // 2) + s * (KT // 2) + (ADA_FRONT + n) // 2 + 1))
                    ada_tile(n % KT, ada_raw[:, n % 2, :], l * ADA_LAYER + ADA_FIRST + ADA_FRONT + s * KT + n)

            def mlp_part(l, s, end):
                count = region(l * (DVE_FRONT + SUPERS * DVE_SUPER) + DVE_PROLOGUE + DVE_FRONT + s * DVE_SUPER,
                               DVE_SUPER)
                at = l * PIECES + FRONT + s * SUPER
                for q in range(2, end):
                    if q == SUPER - 1:
                        cols, bias_cols = dve.snap(s * 8), dve.snap(l * -96 + s * 8 + 96)
                        ada_out(ada_A[:, bass.ds(cols, 8)],
                                bcols[:].rearrange("p l n -> p (l n)")[:, bass.ds(bias_cols, 8)],
                                l * T_LAYER + T_PROLOGUE + T_FRONT + (s + 1) * T_SUPER)
                    mlp_piece(l, s, q)
                    j, p = q // 8 - 1, q % 8
                    if 0 <= j < 4 and p in (3, 5):
                        t = (p - 3) // 2
                        kt = 4 * j + 2 * t
                        splits = l * SPLIT_LAYER + SPLIT_FRONT + s * 8 + 2 * j + t
                        dve.wait_ge(v_hi, splits + 1)
                        v.tensor_tensor(uT_lo[:, kt:kt + 2, :], v_half(j, t), uT_hi[:, kt:kt + 2, :].bitcast(F32),
                                        ALU.subtract).then_inc(split_done, 1)
                    if 4 <= j and p == 1:
                        dve.wait_ge(piece_used, at + 8 * (j + 1) + RING)
                        residual(acc[j % 2], GTM, j - 4, acc_free[j % 2])
                if end == SUPER:
                    dve.wait_ge(piece_used, at + SUPER + RING)
                    residual(acc[1], GTM, 3, acc_free[1])
                close(count)

            with dve.Fori(0, LAYERS) as l:
                count = region(l * (DVE_FRONT + SUPERS * DVE_SUPER) + DVE_PROLOGUE, DVE_FRONT)
                v.tensor_copy(g[:], gcols[:, bass.ds(l * GAINS, GAINS)])
                v.tensor_copy(g_fb, fbias[:].rearrange("p l h -> p (l h)")[:, bass.ds(l * 4, 4)])
                v.tensor_copy(pos_l[:].rearrange("p k s -> p (k s)"),
                              posT[:].rearrange("p l k s -> p (l k s)")[:, bass.ds(l * 64, 64)])
                link(v.tensor_copy(bcur[:], bcols[:].rearrange("p l n -> p (l n)")[:, bass.ds(l * 96 + 32, 64)]))
                link(v.tensor_scalar_add(mscale[:], ada_A[:, 16:32], 1.0))
                v.tensor_tensor(mscale[:], mscale[:], g[:, G_MIX:G_MIX + 16], ALU.mult)
                mean_square(l, "n1", D)
                fill_norm(l, "n1", 0)
                for n in N1T:
                    t_out(l, n)
                    for q in N1_PIECES[n]:
                        side_piece(l, q)
                for q in range(N1_PIECES[N1T[-1]][-1] + 1, FRONT):
                    side_piece(l, q)
                link(v.tensor_scalar_add(mscale[:], ada_B[:, 32:48], 1.0))
                v.tensor_tensor(mscale[:], mscale[:], g[:, G_MLP:G_MLP + 16], ALU.mult)
                evac(l, "wo3")
                dve.wait_ge(acc_free[1], l * PCHUNKS + len(CHUNKS) // 2 + 1)
                dve.sem_inc(rms_src, 1)
                mean_square(l, "n2", D)
                fill_norm(l, "n2", 0)
                for n in N2T:
                    t_out(l, n)
                    if n in ("n2_6", "n2_7"):
                        mlp_piece(l, 0, N2T.index(n) - 6)
                close(count)
                with dve.Fori(0, SUPERS - 1) as s:
                    mlp_part(l, s, SUPER + 2)
                mlp_part(l, SUPERS - 1, SUPER)
                dve.wait_ge(acc_free[1], l * PCHUNKS + len(CHUNKS) // 2 + SUPERS * 4 + 1)
                dve.sem_inc(rms_src, 1)
            mean_square(LAYERS, "final", D)
            dve.wait_ge(fn_landed, 16)
            for m in range(2):
                ins = v.scalar_tensor_tensor(X[:, m, :], X[:, m, :], rstd[:, m:m + 1], FNB, ALU.mult, ALU.mult)
            ins.then_inc(out_ready, 1)

        @block.tensor
        def _(pe):
            pe.sem_inc(piece_used, RING)
            pe.sem_inc(acc_free[0], 1)
            pe.sem_inc(acc_free[1], 1)
            pe.wait_ge(consts, 1)
            pe.wait_ge(packed, 16 * (8 * LAYERS + 1))
            for n, rows in enumerate((LAYERS * GAINS + KT, 96, 96, P)):
                if n:
                    pe.wait_ge(t_free, n)
                pe.transpose(T512[:, 0:rows], diag[0:rows, n, 0:P], ident[0:rows, 0:rows]).then_inc(t_full, 1)

            def t_begin(t):
                pe.wait_ge(t_free, t)

            def ada_sum(t, tiles):
                t_begin(t)
                pe.wait_ge(ada_used, tiles + FIRST_RING)
                for k in range(8):
                    mm = pe.matmul(T512[:, k:k + 1], ada_acc[:, P * k:P * k + P], ones[:, 0:1], start=True, stop=True)
                mm.then_inc(t_full, 1)

            with pe.Fori(0, SUPERS) as b:
                ada_sum(b + PACKS, b * KT + KT)

            def product(a_, at, q, p, n, per, st_hi, st_lo, k0, first, last):
                pe.wait_ge(lo_done, at + q + 1 + RING)
                for k in range(per):
                    wh, wl = w_hi[:, q % RING, k, 0:n], w_lo[:, q % RING, k, 0:n]
                    kt = k0 + k
                    for m in range(2):
                        tok = slice(P * m, P * m + P)
                        o = a_[:, m, 0:n]
                        pe.matmul(o, st_hi[:, kt, tok], wh, start=first and k == 0, stop=False)
                        pe.matmul(o, st_lo[:, kt, tok], wh, start=False, stop=False)
                        mm = pe.matmul(o, st_hi[:, kt, tok], wl, start=False, stop=last and k == per - 1)
                mm.then_inc(piece_used, 1)

            def turn(l, t, blocks, ready=None):
                t_begin(t)
                if ready is not None:
                    pe.wait_ge(*ready)
                for k, halves in enumerate(blocks):
                    for m in range(2):
                        mm = pe.transpose(bank_T[:, k, P * m:P * m + P], halves[m], ident[:])
                mm.then_inc(t_full, 1)

            def from_y(l, name, cols):
                y = y_slot(Y_NO[name])
                return [[y[:, m, c0:c0 + P] for m in range(2)] for c0 in cols]

            Y_SOURCE = {"nqa0": ("nqa", (0, 128)), "nqa1": ("nqa", (256,)), "fq0": ("fq", (0, 128)),
                        "fq1": ("fq", (256, 384)), "fk0": ("fk", (0, 128)), "fk1": ("fk", (256, 384)),
                        "cq0": ("cq", (0, 128)), "cq1": ("cq", (256, 384)), "ckv0": ("ckv", (0, 128)),
                        "kr": ("ckv", (256,)), "nqb0": ("nqb", (0, 128)), "nqb1": ("nqb", (256, 384)),
                        "uq0n": ("uq0", (0, 128)), "uq0r": ("uq0", (256,)), "nq7": ("kc", (0,)),
                        "kcT": ("kc", (128, 256)), "uq1n": ("uq1", (0, 128)), "uq1r": ("uq1", (256,)),
                        "vcT": ("vc", (0, 128)), "ks": ("vc", (256, 384)), "k0": ("kv0", (0, 128)),
                        "kw": ("vs", (0, 128)), "k1": ("kv1", (0, 128))}

            def t_in(l, name):
                t = layer_t(l, T_NO[name]) - 1
                if name[:3] in ("n1_", "n2_"):
                    k = int(name[3:])
                    yn = f"{name[:2]}y{k // 2}"
                    turn(l, t, from_y(l, yn, [256 * (k % 2), 256 * (k % 2) + 128]),
                         (y_full, l * Y_LAYER + Y_NO[yn] + 1))
                elif name in Y_SOURCE:
                    yn, cols = Y_SOURCE[name]
                    turn(l, t, from_y(l, yn, cols), (y_full, l * Y_LAYER + Y_NO[yn] + 1))
                elif name[:4] in ("ofox", "omla", "onsa"):
                    j = int(name[-1])
                    i = ("ofox", "omla", "onsa").index(name[:4])
                    o = (O_FOX, O_MLA, ONSA)[i]
                    turn(l, t, [[o[:, h, m, :] for m in range(2)] for h in (2 * j, 2 * j + 1)],
                         (o_ready, l * 3 + i + 1))
                elif name.startswith("ada"):
                    ada_sum(t, l * ADA_LAYER + SUPERS * KT + KT * (int(name[3:]) + 1))
                elif name == "cum":
                    t_begin(t)
                    pe.wait_ge(fl, l + 1)
                    pe.matmul(bank_T[0:4, 0, 0:128], lf[:, 0, :], tri[:], start=True, stop=True)
                    pe.matmul(bank_T[0:4, 0, 128:256], lf[:, 0, :], ones[:], start=True, stop=False)
                    pe.matmul(bank_T[0:4, 0, 128:256], lf[:, 1, :], tri[:], start=False, stop=True).then_inc(t_full, 1)
                elif name in ("hid0", "hid1"):
                    t_begin(t)
                    if name == "hid0":
                        pe.wait_ge(hpre_done, l + 1)
                    else:
                        pe.wait_ge(acc_free[CI["cw1"] % 2], l * PCHUNKS + CI["cw1"] // 2 + 2)
                    for j in range(4):
                        mm = pe.matmul(T512[:, 32 * j:32 * j + 32], hpre[:, P * j:P * j + P], I2[:], start=True, stop=True)
                    mm.then_inc(t_full, 1)
                elif name == "kcmp":
                    t_begin(t)
                    pe.wait_ge(hid_done, 2 * l + 1)
                    pe.wait_ge(cw2_landed, 32 * l + 32)
                    for j in range(4):
                        mm = pe.matmul(T512[:, 0:32], cw2[0][:, j, :], hid[:, j, :], start=j == 0, stop=j == 3)
                    mm.then_inc(t_full, 1)
                elif name == "vcmp":
                    t_begin(t)
                    pe.wait_ge(hid_done, 2 * l + 2)
                    for j in range(4):
                        mm = pe.matmul(T512[0:32, 0:128], hid[:, j, :], cw2[1][:, j, :], start=j == 0, stop=j == 3)
                    mm.then_inc(t_full, 1)
                elif name == "vrep":
                    t_begin(t)
                    pe.matmul(T512[:, 0:128], Rsel[:], vcmp, start=True, stop=True).then_inc(t_full, 1)
                elif name == "csc":
                    t_begin(t)
                    for m in range(2):
                        for h in range(8):
                            o = 128 * m + 16 * h
                            mm = pe.matmul(T512[:, o:o + 16], NQ[:, h, P * m:P * m + P],
                                           kcmp[:, 16 * (h // 4):16 * (h // 4) + 16], start=True, stop=True)
                    mm.then_inc(t_full, 1)
                elif name == "cpt":
                    t_begin(t)
                    pe.wait_ge(cmp_p, l + 1)
                    for m in range(2):
                        mm = pe.transpose(T512[:, P * m:P * m + P], cs[:, P * m:P * m + P], ident[:])
                    mm.then_inc(t_full, 1)
                elif name[:2] == "co":
                    m, half = int(name[2:]) // 2, int(name[2:]) % 2
                    t_begin(t)
                    pe.matmul(T512, cpt[:, m, :], VBD[:, 4 * half:4 * half + 4, :].rearrange("p h n -> p (h n)"),
                              start=True, stop=True).then_inc(t_full, 1)
                else:
                    n = GATE_ROWS.index(name)
                    t_begin(t)
                    pe.wait_ge(diag_done, 8 * l + n + 1)
                    pe.matmul(T512, ones[:], diag[:, 2 + n % 2, :], start=True, stop=True).then_inc(t_full, 1)

            def scores(l, u):
                kind, h = UNITS[u]
                if u:
                    pe.wait_ge(s_exp, l * NU + u)
                if UNITS[u][1] == 0:
                    pe.wait_ge(t_free, layer_t(l, T_NO[{"slc": "ks", "win": "kw", "fox": "fk1", "mla": "k1"}[kind]]))
                for m in range(2):
                    qt = slice(P * m, P * m + P)
                    keys = P * (m + 1)
                    o = bank_S[:, 0, :] if m == 0 else bank_S[:, 1:3, :].rearrange("p a t -> p (a t)")
                    if kind == "fox":
                        pe.matmul(o, FQ[:, h, qt], FK[:, h, 0:keys], start=True, stop=False)
                        onehot = ident[0:4, h:h + 1]
                        pe.matmul(o, cum[:, qt], onehot.broadcast_to([4, keys]), start=False, stop=False)
                        mm = pe.matmul(o, nident[:, h:h + 1].broadcast_to([4, P]), cum[:, 0:keys], start=False, stop=True)
                    elif kind == "mla":
                        r = 64 * (h % 2)
                        pe.matmul(o, MQ[:, h, qt], MK[:, h, 0:keys], start=True, stop=False)
                        mm = pe.matmul(o, MQR[r:r + 64, h // 2, qt], MKR[r:r + 64, 0:keys], start=False, stop=True)
                    else:
                        k_ = KS if kind == "slc" else KW
                        mm = pe.matmul(o, NQ[:, h, qt], k_[:, h // 4, 0:keys], start=True, stop=True)
                mm.then_inc(s_scores, 1)

            def probs_t(l, u):
                pe.wait_ge(s_exp, l * NU + u + 1)
                if u:
                    pe.wait_ge(s_ptev, l * NU + u)
                for k in range(3):
                    mm = pe.transpose(bank_PT[:, k, :], Pb[:, u % 2, P * k:P * k + P], ident[:])
                mm.then_inc(s_pt, 1)

            def values(l, u):
                kind, h = UNITS[u]
                pe.wait_ge(s_ptev, l * NU + u + 1)
                if u:
                    pe.wait_ge(s_oev, l * NU + u)
                if h == 0 and kind != "mla":
                    i = CI[{"slc": "vs", "win": "vw", "fox": "fv"}[kind]]
                    pe.wait_ge(acc_free[i % 2], l * PCHUNKS + i // 2 + 2)
                V, c0 = {"fox": (FV, P * h), "mla": (MV, P * h), "slc": (VS, P * (h // 4)), "win": (VW, P * (h // 4))}[kind]
                v0, v1 = V[:, 0, c0:c0 + P], V[:, 1, c0:c0 + P]
                pt = PTb[:, u % 2, :]
                pe.matmul(bank_O[:, 0, 0:P], pt[:, 0:P], v0, start=True, stop=True)
                pe.matmul(bank_O[:, 1, 0:P], pt[:, P:2 * P], v0, start=True, stop=False)
                pe.matmul(bank_O[:, 1, 0:P], pt[:, 2 * P:3 * P], v1, start=False, stop=True).then_inc(s_pv, 1)

            def slot(l, s):
                if s >= 2 and SLOTS[s - 2] is not None:
                    values(l, SLOTS[s - 2])
                if SLOTS[s] is not None:
                    scores(l, SLOTS[s])
                if s >= 1 and SLOTS[s - 1] is not None:
                    probs_t(l, SLOTS[s - 1])

            with pe.Fori(0, LAYERS) as l:
                t_in(l, "n1_0")
                for i, (name, w, c0, n, kts, per) in enumerate(CHUNKS):
                    a_ = acc[i % 2]
                    splits = l * SPLIT_LAYER + 1
                    if name in ("wo0b", "wo1b"):
                        pe.sem_inc(acc_free[i % 2], 1)
                    else:
                        pe.wait_ge(acc_free[i % 2], l * PCHUNKS + i // 2 + 1)
                    for p in range(NPIECES[i]):
                        q = FIRST[i] + p
                        if name == "nqa":
                            if p + 1 < 8:
                                t_in(l, f"n1_{p + 1}")
                            pe.wait_ge(split_done, splits + SPLIT_NO[f"n1_{p}"])
                        if name == "uq0" and p == 0:
                            pe.wait_ge(split_done, splits + SPLIT_NO["cq1"])
                        if name == "kv0" and p == 0:
                            pe.wait_ge(split_done, splits + SPLIT_NO["ckv0"])
                        if name == "wo0a" and p in (0, 2):
                            pe.wait_ge(split_done, splits + SPLIT_NO["omla1" if p else "ofox1"])
                        if name == "wo0b" and p == 0:
                            pe.wait_ge(split_done, splits + SPLIT_NO["onsa3"])
                        if name == "cw1":
                            j = p // 16
                            if p % 16 == 0:
                                pe.wait_ge(split_done, splits + SPLIT_NO[("kcT", "vcT")[j]])
                            pe.wait_ge(lo_done, l * PIECES + q + 1 + RING)
                            for k in range(2):
                                kt = (p % 16) * 2 + k
                                st = BLK[j][:, 64 * kt:64 * kt + P]
                                pe.matmul(a_[:, j, :], st, w_hi[:, q % RING, k, :], start=kt == 0, stop=False)
                                mm = pe.matmul(a_[:, j, :], st, w_lo[:, q % RING, k, :], start=False, stop=kt == 31)
                            mm.then_inc(piece_used, 1)
                        else:
                            st, k0 = {"w_in": ((hT_hi, hT_lo), 0), "w_out": ((hT_hi, hT_lo), 0), "uq": ((uT_hi, uT_lo), 0),
                                      "ukv": ((uT_hi, uT_lo), 4)}[w]
                            product(a_, l * PIECES, q, p, n, per, st[0], st[1], k0 + block_of(name, w, p, per),
                                    p == 0 and name not in ("wo0b", "wo1b"), p == NPIECES[i] - 1 and name not in ("wo0a", "wo1a"))
                        for kind, what in STEPS_PE.get(q, []):
                            if kind == "T":
                                t_in(l, what)
                            else:
                                slot(l, what)
                for name in N2T:
                    t_in(l, name)
                with pe.Fori(0, SUPERS) as s:
                    at = l * PIECES + FRONT + s * SUPER
                    t0 = l * T_LAYER + T_PROLOGUE + T_FRONT + s * T_SUPER
                    for ch in range(MLP_CHUNKS):
                        a_ = acc[ch % 2]
                        pe.wait_ge(acc_free[ch % 2], l * PCHUNKS + s * 4 + (len(CHUNKS) + ch) // 2 + 1)
                        for p in range(8):
                            q = ch * 8 + p
                            if q == 0:
                                pe.wait_ge(split_done, l * SPLIT_LAYER + SPLIT_FRONT)
                            st = (hT_hi, hT_lo) if ch < 4 else (uT_hi, uT_lo)
                            if ch == 4:
                                pe.wait_ge(split_done, l * SPLIT_LAYER + SPLIT_FRONT + s * 8 + p + 1)
                            product(a_, at, q, p, 512, 2, st[0], st[1], 2 * p, p == 0, p == 7)
                            j = ch - 1
                            if 0 <= j < 4 and p in (1, 3):
                                t = (p - 1) // 2
                                y = y_slot(j)
                                turn(l, t0 + 2 * j + t,
                                     [[y[:, m, c_:c_ + P] for m in range(2)] for c_ in (256 * t, 256 * t + P)],
                                     (y_full, l * Y_LAYER + Y_FRONT + s * 4 + j + 1))
                            if ch == 7 and p == 5:
                                ada_sum(t0 + 8, l * ADA_LAYER + SUPERS * KT + ADA_FRONT + s * KT + KT)


_INS = ["x", "c", "positions", "inv_freq", "ada_w", "ada_b", "norm_mix", "norm_mlp", "w_in", "fox_b_f", "mla_q_norm",
        "mla_w_uq", "mla_kv_norm", "mla_w_ukv", "nsa_pos_k", "nsa_pos_v", "nsa_cmp_k_w1", "nsa_cmp_k_w2",
        "nsa_cmp_v_w1", "nsa_cmp_v_w2", "out_norm", "w_out", "mlp_w1", "mlp_w2", "final_norm"]


def kernel(**inputs):
    import concourse.bacc as bacc
    from concourse.bass_utils import run_bass_kernel_spmd

    freq = (THETA ** (-np.arange(32) / 32.0)).astype(np.float32).reshape(1, 32)
    nc = bacc.Bacc("TRN2", target_bir_lowering=False, num_devices=1)
    arrays, args = {}, []
    for name in _INS:
        a = freq if name == "inv_freq" else np.ascontiguousarray(inputs[name])
        arrays[f"in_{name}"] = a
        args.append(nc.dram_tensor(f"in_{name}", a.shape, mybir.dt.from_np(a.dtype), kind="ExternalInput").ap())
    args.append(nc.dram_tensor("result", (1, SEQ, D), F32, kind="ExternalOutput").ap())
    trunk(nc, *args)
    r = run_bass_kernel_spmd(nc, [arrays], core_ids=[0])
    return r.results[0]["result"]
```
